# Optimizing a Trainium2 kernel written in Bass

```python
import math
import jax, jax.numpy as jnp
from jax import lax
import numpy as np

D_MODEL = 2048
BATCH = 1
SEQ = 256
DEPTH = 1

CHUNK = 64
N_MIXERS = 3
HEAD_DIM = 64
ROPE_THETA = 10000.0
MAX_START_FRAME = 4096
RMS_EPS = 1e-6
SUBLN_EPS = 1e-5
MASK_VALUE = -1e30
SWA_WINDOW = 128
SWA_WINDOW_CHUNKS = SWA_WINDOW // CHUNK
SWA_Q_HEADS = D_MODEL // HEAD_DIM
SWA_KV_HEADS = 8
SWA_GROUP = SWA_Q_HEADS // SWA_KV_HEADS
DIFF_HEADS = D_MODEL // (2 * HEAD_DIM)
DIFF_Q_BLOCK = 128
RWKV_HEAD = 64
RWKV_HEADS = D_MODEL // RWKV_HEAD
RWKV_DECAY_LORA = 96
RWKV_AAA_LORA = 96
RWKV_GATE_LORA = 256
RWKV_LNX_EPS = 64e-5
FFN_HIDDEN = ((8 * D_MODEL // 3 + 255) // 256) * 256
N_SWA_LAYERS = (DEPTH + N_MIXERS - 1) // N_MIXERS
N_DIFF_LAYERS = (DEPTH + N_MIXERS - 2) // N_MIXERS
N_RWKV_LAYERS = DEPTH // N_MIXERS

kernel_name = "hybrid_swa_diff_rwkv7_adaln_sandwich"

def rms_norm(x, g, eps=RMS_EPS):
    xf = x.astype(jnp.float32)
    y = xf * lax.rsqrt(jnp.mean(xf * xf, axis=-1, keepdims=True) + eps)
    return (y * g.astype(jnp.float32)).astype(x.dtype)

def rope_tables(positions):
    inv_freq = 1.0 / (ROPE_THETA ** (jnp.arange(0, HEAD_DIM, 2, dtype=jnp.float32) / HEAD_DIM))
    ang = positions.astype(jnp.float32)[..., None] * inv_freq
    return jnp.cos(ang)[:, :, None, :], jnp.sin(ang)[:, :, None, :]

def apply_rope(x, cos, sin):
    x1, x2 = jnp.split(x.astype(jnp.float32), 2, axis=-1)
    return jnp.concatenate([x1 * cos - x2 * sin, x2 * cos + x1 * sin], axis=-1).astype(x.dtype)

def swa_sink_attention(h, w_qkv, w_o, sinks, cos, sin):
    B, T, _ = h.shape
    nc = T // CHUNK
    dq = SWA_Q_HEADS * HEAD_DIM
    dkv = SWA_KV_HEADS * HEAD_DIM
    qkv = h @ w_qkv
    q = qkv[..., :dq].reshape(B, T, SWA_Q_HEADS, HEAD_DIM)
    k = qkv[..., dq:dq + dkv].reshape(B, T, SWA_KV_HEADS, HEAD_DIM)
    v = qkv[..., dq + dkv:].reshape(B, T, SWA_KV_HEADS, HEAD_DIM)
    q = apply_rope(q, cos, sin) * (HEAD_DIM ** -0.5)
    k = apply_rope(k, cos, sin)
    qb = q.reshape(B, nc, CHUNK, SWA_KV_HEADS, SWA_GROUP, HEAD_DIM)
    kb = k.reshape(B, nc, CHUNK, SWA_KV_HEADS, HEAD_DIM)
    vb = v.reshape(B, nc, CHUNK, SWA_KV_HEADS, HEAD_DIM)

    def band(t):
        parts = [jnp.pad(t, ((0, 0), (j, 0), (0, 0), (0, 0), (0, 0)))[:, :nc]
                 for j in range(SWA_WINDOW_CHUNKS - 1, -1, -1)]
        return jnp.concatenate(parts, axis=2)

    k_band, v_band = band(kb), band(vb)
    s = jnp.einsum('bnqhgd,bnkhd->bnhgqk', qb, k_band, preferred_element_type=jnp.float32)
    slot_chunk = jnp.arange(SWA_WINDOW_CHUNKS * CHUNK) // CHUNK
    key_chunk = jnp.arange(nc)[:, None] - (SWA_WINDOW_CHUNKS - 1 - slot_chunk)[None, :]
    s = jnp.where((key_chunk >= 0)[None, :, None, None, None, :], s, MASK_VALUE)
    sink = sinks.astype(jnp.float32).reshape(SWA_KV_HEADS, SWA_GROUP)[None, None, :, :, None, None]
    sink = jnp.broadcast_to(sink, s.shape[:-1] + (1,))
    p = jax.nn.softmax(jnp.concatenate([s, sink], axis=-1), axis=-1)[..., :-1]
    o = jnp.einsum('bnhgqk,bnkhd->bnqhgd', p.astype(v_band.dtype), v_band)
    return o.reshape(B, T, dq) @ w_o

def diff_attention(h, w_qkv, w_o, lam, subln_g, cos, sin, layer_idx):
    B, T, _ = h.shape
    H = DIFF_HEADS
    q, k, v = jnp.split(h @ w_qkv, 3, axis=-1)
    q = apply_rope(q.reshape(B, T, 2 * H, HEAD_DIM), cos, sin) * (HEAD_DIM ** -0.5)
    k = apply_rope(k.reshape(B, T, 2 * H, HEAD_DIM), cos, sin)
    v = v.reshape(B, T, H, 2 * HEAD_DIM)
    lam_init = 0.8 - 0.6 * math.exp(-0.3 * layer_idx)
    lf = lam.astype(jnp.float32)
    lam_full = jnp.exp(jnp.sum(lf[0] * lf[1])) - jnp.exp(jnp.sum(lf[2] * lf[3])) + lam_init
    key_chunk = jnp.arange(T) // CHUNK
    nq = T // DIFF_Q_BLOCK
    q_blocks = jnp.moveaxis(q.reshape(B, nq, DIFF_Q_BLOCK, 2 * H, HEAD_DIM), 1, 0)

    def block(args):
        qb, blk = args
        s = jnp.einsum('bqhd,bkhd->bhqk', qb, k, preferred_element_type=jnp.float32)
        q_chunk = (blk * DIFF_Q_BLOCK + jnp.arange(DIFF_Q_BLOCK)) // CHUNK
        s = jnp.where(key_chunk[None, :] <= q_chunk[:, None], s, MASK_VALUE)
        p = jax.nn.softmax(s, axis=-1).reshape(B, H, 2, DIFF_Q_BLOCK, T)
        a = p[:, :, 0] - lam_full * p[:, :, 1]
        return jnp.einsum('bhqk,bkhe->bqhe', a.astype(v.dtype), v)

    o = lax.map(block, (q_blocks, jnp.arange(nq)))
    o = jnp.moveaxis(o, 0, 1).reshape(B, T, H, 2 * HEAD_DIM)
    o = rms_norm(o, subln_g, SUBLN_EPS) * (1.0 - lam_init)
    return o.reshape(B, T, H * 2 * HEAD_DIM) @ w_o

def rwkv7_time_mix(h, mu, w_rkv, w_o, w0, w1, w2, a0, a1, a2, g1, g2, k_k, k_a, r_k, lnx_g, lnx_b):
    B, T, D = h.shape
    H, N = RWKV_HEADS, RWKV_HEAD
    xx = jnp.pad(h, ((0, 0), (1, 0), (0, 0)))[:, :-1] - h
    xr, xw, xk, xv, xa, xg = [h + xx * mu[i] for i in range(6)]
    r = xr @ w_rkv[0]
    k = xk @ w_rkv[1]
    v = xv @ w_rkv[2]
    w = -jax.nn.softplus(-(w0 + jnp.tanh(xw @ w1) @ w2).astype(jnp.float32)) - 0.5
    decay = jnp.exp(-jnp.exp(w))
    a = jax.nn.sigmoid((a0 + (xa @ a1) @ a2).astype(jnp.float32))
    g = jax.nn.sigmoid(xg @ g1) @ g2
    kk = (k * k_k).astype(jnp.float32).reshape(B, T, H, N)
    kk = kk / jnp.maximum(jnp.linalg.norm(kk, axis=-1, keepdims=True), 1e-12)
    k = k.astype(jnp.float32) * (1.0 + (a - 1.0) * k_a.astype(jnp.float32))

    def heads(t):
        return t.astype(jnp.float32).reshape(B, T, H, N)

    rf, kf, vf = heads(r), heads(k), heads(v)

    def step(S, inp):
        r_t, w_t, k_t, v_t, kk_t, a_t = inp
        sa = jnp.einsum('bhij,bhj->bhi', S, -kk_t)
        S = (S * w_t[:, :, None, :] + sa[..., None] * (kk_t * a_t)[:, :, None, :]
             + v_t[..., None] * k_t[:, :, None, :])
        return S, jnp.einsum('bhij,bhj->bhi', S, r_t)

    tm = lambda t: jnp.moveaxis(t, 1, 0)
    S0 = jnp.zeros((B, H, N, N), jnp.float32)
    _, y = lax.scan(step, S0, (tm(rf), tm(heads(decay)), tm(kf), tm(vf), tm(kk), tm(heads(a))))
    y = jnp.moveaxis(y, 0, 1)
    mean = jnp.mean(y, axis=-1, keepdims=True)
    var = jnp.mean(jnp.square(y - mean), axis=-1, keepdims=True)
    yn = ((y - mean) * lax.rsqrt(var + RWKV_LNX_EPS)).reshape(B, T, D) * lnx_g + lnx_b
    bonus = (jnp.sum(rf * kf * r_k, axis=-1, keepdims=True) * vf).reshape(B, T, D)
    return ((yn + bonus).astype(h.dtype) * g) @ w_o

def swiglu(h, w_in, w_out):
    gate, up = jnp.split(h @ w_in, 2, axis=-1)
    return (jax.nn.silu(gate) * up) @ w_out

def setup_inputs(seed: int = 0) -> dict:
    key = jax.random.key(seed)
    keys = iter(jax.random.split(key, 40))
    f32 = jnp.float32
    D, F = D_MODEL, FFN_HIDDEN

    def nrm(shape, scale):
        return jax.random.normal(next(keys), shape, f32) * scale

    x = nrm((BATCH, SEQ, D), 1.0)
    c = nrm((BATCH, D), 1.0)
    start = jax.random.randint(next(keys), (BATCH, 1), 0, MAX_START_FRAME, dtype=jnp.int32)
    positions = start + jnp.arange(SEQ, dtype=jnp.int32)[None, :]
    na, nb, ncc = N_SWA_LAYERS, N_DIFF_LAYERS, N_RWKV_LAYERS
    swa_out = (SWA_Q_HEADS + 2 * SWA_KV_HEADS) * HEAD_DIM
    return {
        "x": x,
        "c": c,
        "positions": positions,
        "mod_w": nrm((DEPTH, D, 6 * D), 0.5 * D ** -0.5),
        "mod_b": nrm((DEPTH, 6 * D), 0.02),
        "norm_g": 1.0 + nrm((DEPTH, 4, D), 0.05),
        "ffn_w_in": nrm((DEPTH, D, 2 * F), D ** -0.5),
        "ffn_w_out": nrm((DEPTH, F, D), F ** -0.5),
        "swa_w_qkv": nrm((na, D, swa_out), D ** -0.5),
        "swa_w_o": nrm((na, SWA_Q_HEADS * HEAD_DIM, D), (SWA_Q_HEADS * HEAD_DIM) ** -0.5),
        "swa_sinks": nrm((na, SWA_Q_HEADS), 1.0),
        "diff_w_qkv": nrm((nb, D, 3 * D), D ** -0.5),
        "diff_w_o": nrm((nb, D, D), D ** -0.5),
        "diff_lambda": nrm((nb, 4, HEAD_DIM), 0.1),
        "diff_subln_g": 1.0 + nrm((nb, 2 * HEAD_DIM), 0.05),
        "rwkv_mu": jax.random.uniform(next(keys), (ncc, 6, D), f32),
        "rwkv_w_rkv": nrm((ncc, 3, D, D), D ** -0.5),
        "rwkv_w_o": nrm((ncc, D, D), D ** -0.5),
        "rwkv_w0": jax.random.uniform(next(keys), (ncc, D), f32, minval=-6.0, maxval=-1.0),
        "rwkv_w1": nrm((ncc, D, RWKV_DECAY_LORA), D ** -0.5),
        "rwkv_w2": nrm((ncc, RWKV_DECAY_LORA, D), 0.1 * RWKV_DECAY_LORA ** -0.5),
        "rwkv_a0": nrm((ncc, D), 0.1),
        "rwkv_a1": nrm((ncc, D, RWKV_AAA_LORA), D ** -0.5),
        "rwkv_a2": nrm((ncc, RWKV_AAA_LORA, D), 0.1 * RWKV_AAA_LORA ** -0.5),
        "rwkv_g1": nrm((ncc, D, RWKV_GATE_LORA), D ** -0.5),
        "rwkv_g2": nrm((ncc, RWKV_GATE_LORA, D), RWKV_GATE_LORA ** -0.5),
        "rwkv_k_k": 0.85 + nrm((ncc, D), 0.05),
        "rwkv_k_a": 1.0 + nrm((ncc, D), 0.05),
        "rwkv_r_k": nrm((ncc, RWKV_HEADS, RWKV_HEAD), 0.1),
        "rwkv_lnx_g": 1.0 + nrm((ncc, D), 0.05),
        "rwkv_lnx_b": nrm((ncc, D), 0.02),
    }

def reference(x, c, positions, mod_w, mod_b, norm_g, ffn_w_in, ffn_w_out,
              swa_w_qkv, swa_w_o, swa_sinks,
              diff_w_qkv, diff_w_o, diff_lambda, diff_subln_g,
              rwkv_mu, rwkv_w_rkv, rwkv_w_o, rwkv_w0, rwkv_w1, rwkv_w2,
              rwkv_a0, rwkv_a1, rwkv_a2, rwkv_g1, rwkv_g2,
              rwkv_k_k, rwkv_k_a, rwkv_r_k, rwkv_lnx_g, rwkv_lnx_b):
    cos, sin = rope_tables(positions)
    cond = jax.nn.silu(c)
    for i in range(DEPTH):
        mod = cond @ mod_w[i] + mod_b[i]
        sh_m, sc_m, gt_m, sh_f, sc_f, gt_f = jnp.split(mod[:, None, :], 6, axis=-1)
        h = rms_norm(x, norm_g[i, 0]) * (1.0 + sc_m) + sh_m
        kind, j = i % N_MIXERS, i // N_MIXERS
        if kind == 0:
            y = swa_sink_attention(h, swa_w_qkv[j], swa_w_o[j], swa_sinks[j], cos, sin)
        elif kind == 1:
            y = diff_attention(h, diff_w_qkv[j], diff_w_o[j], diff_lambda[j], diff_subln_g[j],
                               cos, sin, i)
        else:
            y = rwkv7_time_mix(h, rwkv_mu[j], rwkv_w_rkv[j], rwkv_w_o[j], rwkv_w0[j], rwkv_w1[j],
                               rwkv_w2[j], rwkv_a0[j], rwkv_a1[j], rwkv_a2[j], rwkv_g1[j],
                               rwkv_g2[j], rwkv_k_k[j], rwkv_k_a[j], rwkv_r_k[j],
                               rwkv_lnx_g[j], rwkv_lnx_b[j])
        x = x + gt_m * rms_norm(y, norm_g[i, 1])
        h = rms_norm(x, norm_g[i, 2]) * (1.0 + sc_f) + sh_f
        x = x + gt_f * rms_norm(swiglu(h, ffn_w_in[i], ffn_w_out[i]), norm_g[i, 3])
    return x


_drawn_inputs = setup_inputs


def setup_inputs(seed=0):
    import zlib

    import numpy as np

    out = dict(_drawn_inputs(seed))
    spreads = {}
    factors = {'swa_sinks': 8.0}
    for name, (base, spread) in spreads.items():
        noise = np.random.default_rng([zlib.crc32(name.encode()), seed]).standard_normal(out[name].shape)
        drawn = base * np.exp(spread * noise) if base else spread * noise
        out[name] = __import__('jax').numpy.asarray(drawn.astype(out[name].dtype))
    for name, factor in factors.items():
        out[name] = (out[name] * factor).astype(out[name].dtype)
    return out
```

```python
from contextlib import ExitStack

import concourse.bass as bass
from concourse import mybir

P = 128
F32 = mybir.dt.float32
F32R = mybir.dt.float32r
I32 = mybir.dt.int32
ACT = mybir.ActivationFunctionType
ALU = mybir.AluOpType
AX = mybir.AxisListType

D = 2048
T = 256
HB = T // P
KT = D // P
N = 512
NB = D // N
HD = 64
HALF = HD // 2
CHUNK = 64
QH = D // HD
KVH = 8
KVW = KVH * HD
F = 5632
FB = F // N
FT = F // P
SCALE = float(HD) ** -0.5
RMS_EPS = 1e-6
MASKED = -1e30
WP = 4
WRING = 4
SRING = 2
MP = 2
MPN = KT // MP
MRING = 4
G_KV, G_Q0, G_ATT, G_WO, G_F1 = 0, 8, 12, 28, 40
G_F2 = G_F1 + 2 * WP * FB
SH_M, SC_M, GT_M, SH_F, SC_F, GT_F = (NB * n for n in range(6))
PI_IN = 3.1415925
TWO_PI = (6.28125, 0.0019350051879882812, 3.0199188e-07)
ROUND = 12582912.0


def after(q, s, n=1):
    return q + (s + n) // 4, (s + n) % 4


def build(nc, x, cT, pos, invf, mod_w, modbT, gT, w_qkv, w_o, sinks, w_in, w_out, out):
    with ExitStack() as ctx:
        def sb(name, shape, dt=F32):
            return ctx.enter_context(nc.sbuf_tensor(name, shape, dt))

        def sem(name):
            return ctx.enter_context(nc.semaphore(name))

        raw = sb("raw", [P, WRING, WP, N])
        whi = sb("whi", [P, SRING, WP, N], F32R)
        wlo = sb("wlo", [P, SRING, WP, N], F32R)
        mraw = sb("mraw", [P, MRING, MP, N])
        acc = sb("acc", [P, 2, 2, N])
        hThi = sb("hThi", [P, KT, T], F32R)
        hTlo = sb("hTlo", [P, KT, T], F32R)
        ident = sb("ident", [P, P])
        ones = sb("ones", [P, P])
        ccol = sb("ccol", [P, KT])
        gcol = sb("gcol", [P, 4, KT])
        mbias = sb("mbias", [P, 6 * KT])
        modT = sb("modT", [P, 6 * KT])
        acol = sb("acol", [P, KT])
        vcol = sb("vcol", [P, KT])
        ropeC = sb("ropeC", [P, HB, HD])
        ropeS = sb("ropeS", [P, HB, HD])
        mask = sb("mask", [P, 3 * CHUNK])
        sinkp = sb("sinkp", [P, 2 * QH])
        sinkn = sb("sinkn", [P, 2 * QH])
        ssq = sb("ssq", [P, HB, NB])
        stat = sb("stat", [P, 16])
        rstd = sb("rstd", [P, 8])
        mhalf = sb("mhalf", [P, 1])
        kst = sb("kst", [P, HB, 2, 2, HD])
        vst = sb("vst", [P, HB, 2, HD])
        negm = sb("negm", [P, 2, HB, 4])
        esink = sb("esink", [P, 2, HB, 4])
        mx = sb("mx", [P, 2, HB, 4])
        den = sb("den", [P, 2, HB, 4])

        base = (nc.sbuf_base + 31) // 32 * 32
        ctx.enter_context(nc.sbuf_tensor("arena", [P, 80 * 256], F32))

        def at(name, kb, shape, dt=F32):
            return nc.alloc_sbuf_tensor_at(name, shape, dt, offset=base + int(kb * 1024))

        x0 = at("x0", 32, [P, HB, D])
        nT = at("nT", 48, [P, KT, T])
        posi = at("posi", 72, [P, HB], I32)
        posf = at("posf", 73, [P, HB])
        freq = at("freq", 74, [P, HALF])
        oThi = at("oThi", 0, [P, KT, T], F32R)
        oTlo = at("oTlo", 16, [P, KT, T], F32R)
        qs = at("qs", 32, [P, HB, N])
        qr = at("qr", 36, [P, HB, N])
        kr = at("kr", 40, [P, HB, KVW])
        qT = at("qT", 44, [P, 4, T])
        kT = at("kT", 48, [P, 2, T])
        s0 = at("s0", 50, [P, 2, 4, P])
        s1 = at("s1", 54, [P, 2, 4, 2 * P])
        pT = at("pT", 62, [P, 2, 3, 4, P])
        vr = at("vr", 74, [P, HB, KVW])
        rtmp = at("rtmp", 62, [P, HB, N])
        y = at("y", 32, [P, HB, D])
        x1 = at("x1", 48, [P, HB, D])
        grow = at("grow", 64, [P, D])
        diag1 = at("diag1", 72, [P, 8, P])
        junk = at("junk", 76, [P, N])
        hf = at("hf", 76, [P, 2, 4 * P])
        guT = at("guT", 0, [P, FT, T])
        diag3 = at("diag3", 44, [P, 8, P])
        sg = at("sg", 72, [P, HB, N])
        gu = at("gu", 76, [P, HB, N])

        ps = ctx.enter_context(nc.psum_tensor("ps", [P, 8, N], F32))

        w_loaded = [sem(f"w_loaded{s}") for s in range(WRING)]
        hi_done, lo_done, lop_done = sem("hi_done"), sem("lo_done"), sem("lop_done")
        pe_done = sem("pe_done")
        m_loaded = [sem(f"m_loaded{s}") for s in range(MRING)]
        acc_step = sem("acc_step")
        joined, reduced, mod_added = sem("joined"), sem("reduced"), sem("mod_added")
        c_in, k_in, x_in, x1_in = sem("c_in"), sem("k_in"), sem("x_in"), sem("x1_in")
        consts = sem("consts")
        id_zero, id_done = sem("id_zero"), sem("id_done")
        silu_c = sem("silu_c")
        setup = sem("setup")
        sines = sem("sines")
        tables = sem("tables")
        xsq, xms, xrs, xn, xt, nT_done = (sem(n) for n in ("xsq", "xms", "xrs", "xn", "xt", "nT_done"))
        a1, hf_done, hhi_done, h_ready = (sem(n) for n in ("a1", "hf_done", "hhi_done", "h_ready"))
        half_done, half_evac = sem("half_done"), sem("half_evac")
        rope_a, rope_b, rope_c = sem("rope_a"), sem("rope_b"), sem("rope_c")
        zeros, k_staged, v_staged = sem("zeros"), sem("k_staged"), sem("v_staged")
        qk_pe, qT_done, kT_done = sem("qk_pe"), sem("qT_done"), sem("kT_done")
        sc_pe, sc_read, rmax, m_ready, es_sum, es_done = (
            sem(n) for n in ("sc_pe", "sc_read", "rmax", "m_ready", "es_sum", "es_done"))
        p_exp, den_sum, r_ready, p_act, p_pool = (
            sem(n) for n in ("p_exp", "den_sum", "r_ready", "p_act", "p_pool"))
        pt_pe, pt_act, pt_dve = sem("pt_pe"), sem("pt_act"), sem("pt_dve")
        pv_pe, oThi_done, oT_ready = sem("pv_pe"), sem("oThi_done"), sem("oT_ready")
        vc, diag_done, diag_pe, grow_done = sem("vc"), sem("diag_done"), sem("diag_pe"), sem("grow_done")
        ysq, ychain, yms, yrs = sem("ysq"), sem("ychain"), sem("yms"), sem("yrs")
        x1_done, x1sq, n2_done, n2_pe = sem("x1_done"), sem("x1sq"), sem("n2_done"), sem("n2_pe")
        hf2, hhi2, h2_ready, a2 = sem("hf2"), sem("hhi2"), sem("h2_ready"), sem("a2")
        f_half, silu_done, gu_done, gu_pe, guT_done = (
            sem(n) for n in ("f_half", "silu_done", "gu_done", "gu_pe", "guT_done"))
        gk_hi, gk_lo = sem("gk_hi"), sem("gk_lo")
        y2_half, y2sq, y2ms, y2rs, y2_step, stored = (
            sem(n) for n in ("y2_half", "y2sq", "y2ms", "y2rs", "y2_step", "stored"))

        MCOL0, MCOL = 6, 5

        block = ctx.enter_context(nc.Block())

        @block.sync
        def _(sp):
            def load_w(q, s, src, first=False):
                if not first:
                    for done in (hi_done, lo_done, lop_done):
                        sp.wait_ge(done, 4 * q + s - 3)
                sp.dma_start(raw[:, s], src).then_inc(w_loaded[s], 16)

            def load_m(n, j, col=None, first=False):
                if not first:
                    sp.wait_ge(acc_step, MP * (MPN * n + j - 3))
                c = n if col is None else col
                src = mod_w.rearrange("(j t p) n -> j p t n", p=P, t=MP)[j][:, :, bass.ds(c * N, N)]
                sp.dma_start(mraw[:, j % 4], src).then_inc(m_loaded[j % 4], 16)

            def block_src(w, r, col):
                return w.rearrange("(r t p) n -> r p t n", p=P, t=WP)[r][:, :, bass.ds(col, N)]

            sp.dma_start(ccol[:, :], cT).then_inc(c_in, 16)
            for c in range(4):
                for u in range(2):
                    for j in range(MPN):
                        load_m(2 * c + u, j, (SH_M, SC_M)[u] + c, first=c == u == 0 and j < 4)
                for e, col in enumerate((D, D + KVW, 0)):
                    g = 3 * c + e
                    load_w(g // 4, g % 4, block_src(w_qkv, c, col), first=g < 4)
            load_w(3, 0, block_src(w_qkv, 0, N))

            def beside(i, w, cols, n, minis):
                for s in range(4):
                    load_w(*after(i, s), block_src(w[s // 3], (s + 1) % 4, cols[s // 3]))
                    for e in range(4 if minis else 0):
                        load_m(n + s // 2, 4 * (s % 2) + e)

            with sp.Fori(0, 2) as i:
                beside(i + 3, (w_qkv, w_qkv), ((i + 1) * N, (i + 2) * N), 8 + 2 * i, True)
            beside(5, (w_qkv, w_o), (3 * N, 0), 12, True)
            beside(6, (w_o, w_o), (0, N), 14, True)
            with sp.Fori(1, 3) as i:
                beside(6 + i, (w_o, w_o), (i * N, (i + 1) * N), 14 + 2 * i, True)
            beside(9, (w_o, w_in), (3 * N, 0), None, False)
            sp.wait_ge(oT_ready, 8)
            for b in range(HB):
                sp.dma_start(x1[:, b], x[b * P:(b + 1) * P, :]).then_inc(x1_in, 16)
            for s in range(1, 4):
                load_w(10, s, block_src(w_in, s, 0))

            def f1_ahead(i, with_mod):
                for u in range(2):
                    for s in range(4):
                        col = F + i * N if u == 0 else (i + 1) * N
                        load_w(11 + 2 * i + u, s, block_src(w_in, s, col))
                        if with_mod:
                            for j in F_MOD[4 * u + s]:
                                load_m(GT_F - 1 + i, j)

            f1_ahead(0, False)
            with sp.Fori(1, 5) as i:
                f1_ahead(i, True)
            with sp.Fori(5, FB - 1) as i:
                f1_ahead(i, False)
            for s in range(4):
                load_w(11 + 2 * (FB - 1), s, block_src(w_in, s, F + (FB - 1) * N))
            with sp.Fori(0, FT // 4) as i:
                for s in range(4):
                    src = w_out.rearrange("(k s p) (a n) -> s p k a n", p=P, s=4, n=N)[s][:, bass.ds(i, 1)]
                    load_w(G_F2 // 4 + i, s, src)
            for b in range(HB):
                for e in range(2):
                    sp.wait_ge(y2_step, 6 * b + 4 + e + 1)
                    cs = slice(e * D // 2, (e + 1) * D // 2)
                    sp.dma_start(out[b * P:(b + 1) * P, cs], x1[:, b, cs]).then_inc(stored, 16)
            sp.wait_ge(stored, 16 * 2 * HB)

        @block.scalar
        def _(act):
            A = nc.scalar.activation

            def hi(q, s):
                act.wait_ge(w_loaded[s], 16 * (q + 1))
                if not (isinstance(q, int) and 4 * q + s < SRING):
                    act.wait_ge(pe_done, 4 * q + s - 1)
                A(whi[:, s % 2], raw[:, s], ACT.Copy).then_inc(hi_done, 1)

            for dst, src in ((posi, pos), (freq, invf), (gcol, gT), (mbias, modbT), (sinkp, sinks)):
                act.dma_start(dst[:], src).then_inc(k_in, 16)
            for b in range(HB):
                act.dma_start(x0[:, b], x[b * P:(b + 1) * P, :]).then_inc(x_in, 16)
            act.wait_ge(c_in, 16)
            A(ccol[:, :], ccol[:, :], ACT.Silu).then_inc(silu_c, 1)
            act.wait_ge(x_in, 32)
            for b in range(HB):
                A(nT[:, 8 * b:8 * b + 8].rearrange("p k t -> p (k t)"), x0[:, b], ACT.Square,
                  accum_out=ssq[:, b, 0:1]).then_inc(xsq, 1)
            for b in range(HB):
                act.wait_ge(xrs, b + 1)
                A(x0[:, b], x0[:, b], ACT.Copy, scale=rstd[:, b:b + 1]).then_inc(xn, 1)
            for b in range(HB):
                for r in range(4):
                    act.wait_ge(xt, 4 * b + r + 1)
                    A(nT[:, 4 * r:4 * r + 4, b * P:(b + 1) * P],
                      ps[:, 4 * b + r].rearrange("p (k t) -> p k t", t=P), ACT.Copy).then_inc(nT_done, 1)
            act.wait_ge(setup, 12)
            A(ropeC[:, :, 0:HALF], ropeC[:, :, 0:HALF], ACT.Sin).then_inc(sines, 1)
            A(ropeS[:, :, HALF:], ropeS[:, :, HALF:], ACT.Sin).then_inc(sines, 1)

            def half_ready(sig, count, q, b):
                if b == 0:
                    act.wait_ge(sig, count)
                else:
                    act.wait_ge(pe_done, 4 * q + 4)

            for c in range(4):
                act.wait_ge(hf_done, c + 1)
                A(hThi[:, 4 * c:4 * c + 4], nT[:, 4 * c:4 * c + 4], ACT.Copy).then_inc(hhi_done, 1)
                for g in range(3 * c, 3 * c + 3):
                    hi(g // 4, g % 4)
            for e, dst in enumerate((qs, vr, qs)):
                for b in range(HB):
                    act.wait_ge(half_done if b == 0 else pe_done, e + 1 if b == 0 else 10 + e)
                    if e == 2 and b == 0:
                        act.wait_ge(rope_c, 1)
                    A(dst[:, b], ps[:, 2 * e + b], ACT.Copy).then_inc(half_evac, 1)
                if e == 0:
                    hi(3, 0)

            def probs(i):
                for u in range(2):
                    act.wait_ge(m_ready, 2 * i + u + 1)
                    for b in range(HB):
                        for h in range(4):
                            s = s0[:, u, h] if b == 0 else s1[:, u, h, CHUNK:]
                            p = A(s, s, ACT.Exp, bias=negm[:, u, b, h:h + 1], scale=SCALE,
                                  accum_out=den[:, u, b, h:h + 1])
                    p.then_inc(p_exp, 1)
                    act.wait_ge(es_sum, 2 * i + u + 1)
                    A(esink[:, u], esink[:, u], ACT.Exp).then_inc(es_done, 1)

            def normalise(i):
                for u in range(2):
                    act.wait_ge(r_ready, 2 * i + u + 1)
                    for h in range(4):
                        s = s1[:, u, h, CHUNK:]
                        p = A(s, s, ACT.Copy, scale=den[:, u, 1, h:h + 1])
                    p.then_inc(p_act, 1)

            def pT_out(i):
                for u in range(2):
                    for part in (1, 2):
                        act.wait_ge(pt_pe, 6 * i + 3 * u + part + 1)
                        A(pT[:, u, part].rearrange("p h t -> p (h t)"), ps[:, 3 + 2 * u + part],
                          ACT.Copy).then_inc(pt_act, 1)

            def oT_out(i):
                for u in range(2):
                    act.wait_ge(pv_pe, 2 * i + u + 1)
                    A(oThi[:, bass.ds(4 * i + 2 * u, 2)].rearrange("p a t -> p (a t)"), ps[:, 6 + u],
                      ACT.Copy).then_inc(oThi_done, 1)

            def attention(i, first, last):
                q = 3 + i
                hi(*after(q, 0))
                if not first:
                    act.wait_ge(rope_c, i + 2)
                    pT_out(i - 1)
                hi(*after(q, 1))
                for e in range(2):
                    act.wait_ge(qk_pe, 3 * i + e + 1)
                    A(qT[:, 2 * e:2 * e + 2].rearrange("p a t -> p (a t)"), ps[:, 2 + e],
                      ACT.Copy).then_inc(qT_done, 1)
                if not first:
                    oT_out(i - 1)
                hi(*after(q, 2))
                probs(i)
                if not last:
                    hi(*after(q, 3))
                    act.wait_ge(rope_c, i + 2)
                    for b in range(HB):
                        half_ready(half_done, i + 4, q, b)
                        A(qs[:, b], ps[:, b], ACT.Copy).then_inc(half_evac, 1)
                normalise(i)

            def evac_y(w):
                for b in range(HB):
                    half_ready(half_done, 7 + w, 6 + w, b)
                    if not (isinstance(w, int) and w == b == 0):
                        act.wait_ge(ysq, 2 * w + b)
                    A(junk[:, :], ps[:, b], ACT.Square, accum_out=ssq[:, b, bass.ds(w, 1)]).then_inc(ysq, 1)
                    A(y[:, b, bass.ds(w * N, N)], ps[:, b], ACT.Copy).then_inc(half_evac, 1)

            attention(0, True, False)
            with act.Fori(1, 3) as i:
                attention(i, False, False)
            attention(3, False, True)
            pT_out(3)
            oT_out(3)
            hi(7, 0)
            evac_y(0)

            def grow_evac(rnd, b0, n0):
                for e in range(2):
                    act.wait_ge(diag_pe, n0 + 2 * rnd + e + 1)
                    A(grow[:, (2 * rnd + e) * N:(2 * rnd + e + 1) * N], ps[:, b0 + e],
                      ACT.Copy).then_inc(grow_done, 1)

            with act.Fori(1, 3) as w:
                for s in range(4):
                    hi(*after(6 + w, s))
                evac_y(w)
            for s in range(4):
                hi(*after(9, s))
                if s == 0:
                    grow_evac(0, 2, 0)
                if s == 2:
                    grow_evac(1, 2, 0)
            evac_y(3)
            for b in range(HB):
                act.wait_ge(x1_done, b + 1)
                A(y[:, b], x1[:, b], ACT.Square, accum_out=stat[:, b:b + 1]).then_inc(x1sq, 1)
                act.wait_ge(yrs, 2 * b + 2)
                A(y[:, b], x1[:, b], ACT.Copy, scale=rstd[:, 2 + b:3 + b]).then_inc(n2_done, 1)
            for b in range(HB):
                for r in range(4):
                    act.wait_ge(hf2, 4 * b + r + 1)
                    A(hThi[:, 4 * r:4 * r + 4, b * P:(b + 1) * P],
                      hf[:, r % 2].rearrange("p (k t) -> p k t", t=P), ACT.Copy).then_inc(hhi2, 1)

            def f1(i, first, tail):
                q = 10 + 2 * i
                for u in range(2):
                    for s in range(4):
                        if tail and u == 1 and s == 3:
                            gk(0, 0)
                        hi(*after(q + u, s))
                        if u == 0 and s == 1 and not first:
                            act.wait_ge(gu_pe, 2 * i - 1)
                            A(guT[:, bass.ds(4 * i - 4, 4), 0:P],
                              ps[:, 6].rearrange("p (k t) -> p k t", t=P), ACT.Copy).then_inc(guT_done, 1)
                        if u == 0 and s == 3:
                            if not first:
                                act.wait_ge(gu_done, 2 * i)
                            for b in range(HB):
                                half_ready(f_half, 2 * i + 1, q, b)
                                A(sg[:, b], ps[:, b], ACT.Silu).then_inc(silu_done, 1)
                        if tail and u == 1 and s in (0, 2):
                            grow_evac(s // 2, 4, 4)

            def gk(i, s):
                act.wait_ge(pe_done, G_F2 + 4 * i + s - 3)
                if isinstance(i, int) and i == 0 and s == 0:
                    act.wait_ge(guT_done, 2 * (FB - 1))
                A(hThi[:, s], guT[:, bass.ds(4 * i + s, 1)].rearrange("p k t -> p (k t)"),
                  ACT.Copy).then_inc(gk_hi, 1)

            f1(0, True, False)
            with act.Fori(1, FB - 1) as i:
                f1(i, False, False)
            f1(FB - 1, False, True)
            act.wait_ge(gu_pe, 2 * FB - 1)
            A(guT[:, 4 * FB - 4:4 * FB, 0:P], ps[:, 6].rearrange("p (k t) -> p k t", t=P),
              ACT.Copy).then_inc(guT_done, 1)
            q2 = G_F2 // 4

            def f2(i, end=False):
                for s in range(4):
                    if s < 3:
                        gk(i, s + 1)
                        hi(*after(q2 + i, s))
                    elif not end:
                        gk(i + 1, 0)
                        hi(*after(q2 + i, s))

            f2(0)
            with act.Fori(1, FT // 4 - 1) as i:
                f2(i)
            act.wait_ge(guT_done, 2 * FB)
            f2(FT // 4 - 1, end=True)
            for b in range(HB):
                act.wait_ge(y2_half, b + 1)
                A(guT[:, 8 * b:8 * b + 8].rearrange("p k t -> p (k t)"),
                  ps[:, 4 * b:4 * b + 4].rearrange("p a n -> p (a n)"), ACT.Square,
                  accum_out=stat[:, 2 + b:3 + b]).then_inc(y2sq, 1)

        @block.vector
        def _(dve):
            V = nc.vector

            def lo(q, s):
                dve.wait_ge(hi_done, 4 * q + s + 1)
                V.tensor_tensor(wlo[:, s % 2, 0:2], raw[:, s, 0:2], whi[:, s % 2, 0:2].bitcast(F32),
                                ALU.subtract).then_inc(lo_done, 1)

            def mod(n, j, a, waits):
                dve.wait_ge(m_loaded[j % 4], 16 * (2 * n + j // 4 + 1))
                if j == 0 and waits is not None:
                    dve.wait_ge(reduced, waits)
                for t in range(MP):
                    k = MP * j + t
                    c = ccol[:, k:k + 1]
                    if k < 2:
                        ins = V.tensor_scalar(acc[:, a, t], mraw[:, j % 4, t], c, None, ALU.mult)
                    else:
                        dve.wait_ge(acc_step, KT * n + k - 1)
                        ins = V.scalar_tensor_tensor(acc[:, a, t], mraw[:, j % 4, t], c, acc[:, a, t],
                                                     ALU.mult, ALU.add)
                    ins.then_inc(acc_step, 1)

            def mod_add(n, col=None, bank=MCOL):
                c = n if col is None else col
                dve.wait_ge(reduced, n + 1)
                V.tensor_tensor(modT[:, bass.ds(4 * c, 4)], ps[:, bank, 0:4], mbias[:, bass.ds(4 * c, 4)],
                                ALU.add).then_inc(mod_added, 1)

            count = [0]

            def link(ins):
                count[0] += 1
                ins.then_inc(setup, 1)
                dve.wait_ge(setup, count[0])

            V.memset(ones[:, :], 1.0)
            V.memset(mhalf[:, :], -0.5)
            V.memset(mask[0:CHUNK, 0:2 * CHUNK], 0.0)
            V.memset(mask[CHUNK:P, CHUNK:], 0.0)
            V.memset(mask[CHUNK:P, 0:CHUNK], MASKED)
            V.memset(mask[0:CHUNK, 2 * CHUNK:], MASKED).then_inc(consts, 1)
            dve.wait_ge(k_in, 80)
            link(V.tensor_copy(posf[:, :], posi[:, :]))
            link(V.tensor_tensor(ropeS[:, :, HALF:], posf[:, :].unsqueeze(2).broadcast_to([P, HB, HALF]),
                                 freq[:, :].unsqueeze(1).broadcast_to([P, HB, HALF]), ALU.mult))
            link(V.tensor_scalar(sinkn[:, :], sinkp[:, :], -1.0, None, ALU.mult))
            turns = ropeC[:, :, HALF:]
            ang, angc = ropeS[:, :, HALF:], ropeC[:, :, 0:HALF]
            link(V.tensor_scalar(angc, ang, 0.0, None, ALU.add))
            for r, shift in ((ang, 0.0), (angc, 0.25)):
                link(V.tensor_scalar(turns, r, 1.0 / (2.0 * 3.141592653589793), shift, ALU.mult, ALU.add))
                link(V.tensor_scalar(turns, turns, ROUND, -ROUND, ALU.add, ALU.add))
                for part in TWO_PI:
                    link(V.scalar_tensor_tensor(r, turns, -part, r, ALU.mult, ALU.add))
            link(V.tensor_scalar(angc, angc, 1.5707963267948966, PI_IN, ALU.add, ALU.min))
            link(V.tensor_scalar(angc, angc, -PI_IN, None, ALU.max))
            link(V.tensor_scalar(ang, ang, PI_IN, -PI_IN, ALU.min, ALU.max))
            assert count[0] == SETUP_ANGLES
            dve.wait_ge(xsq, 2)
            V.tensor_scalar(stat[:, 12:14], ssq[:, :, 0], 1.0 / D, RMS_EPS, ALU.mult, ALU.add).then_inc(xms, 1)
            dve.wait_ge(silu_c, 1)
            def first_mod(n, js):
                for j in js:
                    mod(n, j, n % 2, n - 1 if n >= 2 else None)

            def modulate(c):
                ks = slice(4 * c, 4 * c + 4)
                mod_add(2 * c + 1, SC_M + c, MCOL0)
                dve.wait_ge(mod_added, 2 * c + 2)
                V.scalar_tensor_tensor(acol[:, ks], modT[:, KT + 4 * c:KT + 4 * c + 4], 1.0, gcol[:, 0, ks],
                                       ALU.add, ALU.mult).then_inc(a1, 1)
                dve.wait_ge(a1, c + 1)
                for k in range(4 * c, 4 * c + 4):
                    ins = V.tensor_scalar(nT[:, k], nT[:, k], acol[:, k:k + 1], modT[:, k:k + 1],
                                          ALU.mult, ALU.add)
                ins.then_inc(hf_done, 1)

            def h_lo(c):
                dve.wait_ge(hhi_done, c + 1)
                V.tensor_tensor(hTlo[:, 4 * c:4 * c + 4], nT[:, 4 * c:4 * c + 4],
                                hThi[:, 4 * c:4 * c + 4].bitcast(F32), ALU.subtract).then_inc(h_ready, 1)

            def rope_parts(n, half_count, dst):
                dve.wait_ge(half_evac, half_count)
                V.tensor_tensor(dst.rearrange("p b (h d) -> p b h d", d=HD),
                                qs[:].rearrange("p b (h d) -> p b h d", d=HD),
                                ropeC[:].unsqueeze(2).broadcast_to([P, HB, 8, HD]), ALU.mult).then_inc(rope_a, 1)
                yield
                dve.wait_ge(rope_a, n + 1)
                dve.wait_ge(rope_b, 2 * n + 2)
                V.tensor_tensor(dst, dst, rtmp[:], ALU.add).then_inc(rope_c, 1)
                yield

            for c in range(4):
                first_mod(2 * c, range(0, 4))
                if c == 0:
                    dve.wait_ge(sines, 2)
                    V.tensor_copy(ropeC[:, :, HALF:], ropeC[:, :, 0:HALF])
                    V.tensor_scalar(ropeS[:, :, 0:HALF], ropeS[:, :, HALF:], -1.0, None,
                                    ALU.mult).then_inc(tables, 1)
                    dve.wait_ge(nT_done, 8)
                else:
                    modulate(c - 1)
                first_mod(2 * c, range(4, 8))
                if c:
                    h_lo(c - 1)
                    for g in (3 * c - 3, 3 * c - 2):
                        lo(g // 4, g % 4)
                first_mod(2 * c + 1, range(0, 4))
                if c:
                    lo((3 * c - 1) // 4, (3 * c - 1) % 4)
                mod_add(2 * c, SH_M + c, MCOL0)
                first_mod(2 * c + 1, range(4, 8))
            modulate(3)
            h_lo(3)
            lo(2, 1)
            lo(2, 2)
            dve.wait_ge(h_ready, 4)
            V.memset(s1[:, :, :, 0:CHUNK], 0.0).then_inc(zeros, 1)
            lo(2, 3)
            keys = rope_parts(0, 2, kr[:])
            next(keys)
            lo(3, 0)
            next(keys)

            def max_and_sinks(i):
                dve.wait_ge(sc_pe, i + 1)
                for u in range(2):
                    V.tensor_tensor(s0[:, u].rearrange("p (e m) k -> p e m k", e=2),
                                    ps[:, 2:4, u * 256:(u + 1) * 256].rearrange("p e (m k) -> p e m k", m=2),
                                    mask[:, CHUNK:].unsqueeze(1).unsqueeze(1).broadcast_to([P, 2, 2, P]),
                                    ALU.add).then_inc(sc_read, 1)
                    V.tensor_tensor(s1[:, u, :, CHUNK:].rearrange("p (e m) k -> p e m k", e=2),
                                    ps[:, 4 + 2 * u:6 + 2 * u, 0:6 * CHUNK].rearrange("p e (m k) -> p e m k", m=2),
                                    mask[:].unsqueeze(1).unsqueeze(1).broadcast_to([P, 2, 2, 3 * CHUNK]),
                                    ALU.add).then_inc(sc_read, 1)
                for u in range(2):
                    dve.wait_ge(sc_read, 4 * i + 2 * u + 2)
                    V.tensor_reduce(mx[:, u, 0], s0[:, u], AX.X, ALU.max).then_inc(rmax, 1)
                    V.tensor_reduce(mx[:, u, 1], s1[:, u, :, CHUNK:], AX.X, ALU.max).then_inc(rmax, 1)
                    dve.wait_ge(rmax, 4 * i + 2 * u + 2)
                    V.scalar_tensor_tensor(negm[:, u].rearrange("p b h -> p (b h)"),
                                           mx[:, u].rearrange("p b h -> p (b h)"), -SCALE,
                                           sinkn[:, bass.ds(16 * i + 8 * u, 8)], ALU.mult,
                                           ALU.min).then_inc(m_ready, 1)
                    dve.wait_ge(m_ready, 2 * i + u + 1)
                    V.tensor_tensor(esink[:, u].rearrange("p b h -> p (b h)"),
                                    negm[:, u].rearrange("p b h -> p (b h)"),
                                    sinkp[:, bass.ds(16 * i + 8 * u, 8)], ALU.add).then_inc(es_sum, 1)

            def denominators(i):
                for u in range(2):
                    dve.wait_ge(p_exp, 2 * i + u + 1)
                    dve.wait_ge(es_done, 2 * i + u + 1)
                    V.tensor_tensor(den[:, u], den[:, u], esink[:, u], ALU.add).then_inc(den_sum, 1)
                for u in range(2):
                    dve.wait_ge(den_sum, 2 * i + u + 1)
                    V.reciprocal(den[:, u], den[:, u]).then_inc(r_ready, 1)

            def pT_out(i):
                for u in range(2):
                    dve.wait_ge(pt_pe, 6 * i + 3 * u + 1)
                    V.tensor_copy(pT[:, u, 0].rearrange("p h t -> p (h t)"), ps[:, 2 + u]).then_inc(pt_dve, 1)

            def oT_lo(i):
                for u in range(2):
                    dve.wait_ge(oThi_done, 2 * i + u + 1)
                    V.tensor_tensor(oTlo[:, bass.ds(4 * i + 2 * u, 2)].rearrange("p a t -> p (a t)"), ps[:, 6 + u],
                                    oThi[:, bass.ds(4 * i + 2 * u, 2)].rearrange("p a t -> p (a t)").bitcast(F32),
                                    ALU.subtract).then_inc(oT_ready, 1)

            def attention(i, first, last):
                q = 3 + i
                m1, m2 = 8 + 2 * i, 9 + 2 * i

                def m(which, *js):
                    for j in js:
                        mod(m1 if which == 1 else m2, j, which - 1, (m1 if which == 1 else m2) - 1)

                turned = rope_parts(1 + i, 2 * (3 + i), qr[:])
                next(turned)
                m(1, 0, 1)
                if not first:
                    mod_add(m1 - 2)
                next(turned)
                lo(*after(q, 0))
                m(1, 2, 3)
                if not first:
                    pT_out(i - 1)
                m(1, 4, 5)
                lo(*after(q, 1))
                m(1, 6)
                dve.wait_ge(qk_pe, 3 * i + 3)
                V.tensor_copy(kT[:].rearrange("p u t -> p (u t)"), ps[:, 4]).then_inc(kT_done, 1)
                m(1, 7)
                if not first:
                    mod_add(m1 - 1)
                m(2, 0, 1)
                if not first:
                    oT_lo(i - 1)
                lo(*after(q, 2))
                m(2, 2)
                max_and_sinks(i)
                m(2, 3, 4)
                if not last:
                    lo(*after(q, 3))
                m(2, 5, 6, 7)
                denominators(i)

            attention(0, True, False)
            with dve.Fori(1, 3) as i:
                attention(i, False, False)
            attention(3, False, True)
            mod_add(14)
            pT_out(3)
            oT_lo(3)
            lo(7, 0)
            mod_add(15)

            V.tensor_tensor(vcol[:, :], modT[:, 2 * KT:3 * KT], gcol[:, 1], ALU.mult).then_inc(vc, 1)
            with dve.Fori(0, 2) as i:
                for s in range(4):
                    lo(*after(7 + i, s))
                    n = 16 + 2 * i + s // 2
                    for e in range(4):
                        mod(n, 4 * (s % 2) + e, s // 2, n - 1)
                    if s == 2:
                        mod_add(n - 1)
                mod_add(n)
            dve.wait_ge(mod_added, 20)
            V.scalar_tensor_tensor(acol[:, :], modT[:, 4 * KT:5 * KT], 1.0, gcol[:, 2], ALU.add,
                                   ALU.mult).then_inc(a2, 1)
            for s in range(4):
                lo(*after(9, s))
            dve.wait_ge(grow_done, 4)
            dve.wait_ge(x1_in, 32)
            for b in range(HB):
                dve.wait_ge(ysq, 7 + b)
                V.tensor_reduce(stat[:, 4 + b:5 + b], ssq[:, b], AX.X, ALU.add).then_inc(ychain, 1)
                dve.wait_ge(ychain, 2 * b + 1)
                V.tensor_scalar(stat[:, 6 + b:7 + b], stat[:, 4 + b:5 + b], 1.0 / D, RMS_EPS, ALU.mult,
                                ALU.add).then_inc(yms, 1)
                dve.wait_ge(half_evac, 19 + b)
                dve.wait_ge(yrs, 2 * b + 1)
                V.scalar_tensor_tensor(y[:, b], y[:, b], rstd[:, b:b + 1], grow[:, :], ALU.mult,
                                       ALU.mult).then_inc(ychain, 1)
                dve.wait_ge(ychain, 2 * b + 2)
                V.tensor_tensor(x1[:, b], x1[:, b], y[:, b], ALU.add).then_inc(x1_done, 1)
                dve.wait_ge(x1sq, b + 1)
                V.tensor_scalar(stat[:, 8 + b:9 + b], stat[:, b:b + 1], 1.0 / D, RMS_EPS, ALU.mult,
                                ALU.add).then_inc(yms, 1)
            dve.wait_ge(a2, 1)

            def h2_mod(b, r):
                dve.wait_ge(n2_pe, 4 * b + r + 1)
                if 4 * b + r >= 2:
                    dve.wait_ge(h2_ready, 4 * b + r - 1)
                bank = H2_BANKS[4 * b + r]
                for t in range(4):
                    k = 4 * r + t
                    ins = V.tensor_scalar(hf[:, r % 2, t * P:(t + 1) * P], ps[:, bank, t * P:(t + 1) * P],
                                          acol[:, k:k + 1], modT[:, 3 * KT + k:3 * KT + k + 1], ALU.mult, ALU.add)
                ins.then_inc(hf2, 1)

            def h2_lo(b, r):
                dve.wait_ge(hhi2, 4 * b + r + 1)
                V.tensor_tensor(hTlo[:, 4 * r:4 * r + 4, b * P:(b + 1) * P],
                                hf[:, r % 2].rearrange("p (k t) -> p k t", t=P),
                                hThi[:, 4 * r:4 * r + 4, b * P:(b + 1) * P].bitcast(F32),
                                ALU.subtract).then_inc(h2_ready, 1)

            steps = [(b, r) for b in range(HB) for r in range(4)]
            h2_mod(*steps[0])
            for n in range(1, 8):
                h2_mod(*steps[n])
                h2_lo(*steps[n - 1])
            h2_lo(*steps[7])

            def f1(i, first, with_mod, tail):
                q = 10 + 2 * i
                for u in range(2):
                    for s in range(4):
                        if tail and u == 1 and s == 3:
                            gk_low(0, 0)
                        lo(*after(q + u, s))
                        if u == 0 and s == 1 and not first:
                            dve.wait_ge(gu_pe, 2 * i)
                            V.tensor_copy(guT[:, bass.ds(4 * i - 4, 4), P:2 * P],
                                          ps[:, 7].rearrange("p (k t) -> p k t", t=P)).then_inc(guT_done, 1)
                        if with_mod:
                            for j in F_MOD[4 * u + s]:
                                mod(GT_F - 1 + i, j, 0, GT_F - 1 + i)
                if with_mod:
                    mod_add(GT_F - 1 + i)
                for b in range(HB):
                    if b == 0:
                        dve.wait_ge(f_half, 2 * i + 2)
                    else:
                        dve.wait_ge(pe_done, 4 * (q + 1) + 4)
                    dve.wait_ge(silu_done, 2 * i + b + 1)
                    V.tensor_tensor(gu[:, b], sg[:, b], ps[:, 2 + b], ALU.mult).then_inc(gu_done, 1)

            def gk_low(i, s):
                dve.wait_ge(gk_hi, 4 * i + s + 1)
                V.tensor_tensor(hTlo[:, s], guT[:, bass.ds(4 * i + s, 1)].rearrange("p k t -> p (k t)"),
                                hThi[:, s].bitcast(F32), ALU.subtract).then_inc(gk_lo, 1)

            f1(0, True, False, False)
            with dve.Fori(1, 5) as i:
                f1(i, False, True, False)
            dve.wait_ge(mod_added, 24)
            dve.wait_ge(diag_done, 2)
            V.tensor_tensor(vcol[:, :], modT[:, 5 * KT:6 * KT], gcol[:, 3], ALU.mult).then_inc(vc, 1)
            with dve.Fori(5, FB - 1) as i:
                f1(i, False, False, False)
            f1(FB - 1, False, False, True)
            dve.wait_ge(gu_pe, 2 * FB)
            V.tensor_copy(guT[:, 4 * FB - 4:4 * FB, P:2 * P],
                          ps[:, 7].rearrange("p (k t) -> p k t", t=P)).then_inc(guT_done, 1)
            q2 = G_F2 // 4

            def f2(i, end=False):
                for s in range(4):
                    if s < 3:
                        gk_low(i, s + 1)
                        lo(*after(q2 + i, s))
                    elif not end:
                        gk_low(i + 1, 0)
                        lo(*after(q2 + i, s))

            f2(0)
            with dve.Fori(1, FT // 4 - 1) as i:
                f2(i)
            f2(FT // 4 - 1, end=True)
            for b in range(HB):
                dve.wait_ge(y2sq, b + 1)
                V.tensor_scalar(stat[:, 10 + b:11 + b], stat[:, 2 + b:3 + b], 1.0 / D, RMS_EPS, ALU.mult,
                                ALU.add).then_inc(y2ms, 1)
                dve.wait_ge(y2rs, b + 1)
                for e in range(4):
                    cs = slice(e * N, (e + 1) * N)
                    V.scalar_tensor_tensor(guT[:, 16 + 2 * e:18 + 2 * e].rearrange("p k t -> p (k t)"),
                                           ps[:, 4 * b + e], rstd[:, 4 + b:5 + b], grow[:, cs], ALU.mult,
                                           ALU.mult).then_inc(y2_step, 1)
                for e in range(2):
                    cs = slice(e * D // 2, (e + 1) * D // 2)
                    dve.wait_ge(y2_step, 6 * b + 2 * e + 2)
                    V.tensor_tensor(x1[:, b, cs], x1[:, b, cs],
                                    guT[:, 16 + 4 * e:20 + 4 * e].rearrange("p k t -> p (k t)"),
                                    ALU.add).then_inc(y2_step, 1)

        @block.gpsimd
        def _(pool):
            G = nc.gpsimd

            def lo(q, s):
                pool.wait_ge(hi_done, 4 * q + s + 1)
                G.tensor_tensor(wlo[:, s % 2, 2:4], raw[:, s, 2:4], whi[:, s % 2, 2:4].bitcast(F32),
                                ALU.subtract).then_inc(lop_done, 1)

            def inv_root(dst, src, done):
                G.tensor_tensor(dst, src, mhalf[:, :], ALU.pow).then_inc(done, 1)

            G.memset(ident[:, :], 0.0).then_inc(id_zero, 1)
            pool.wait_ge(id_zero, 1)
            G.affine_select(out=ident[:, :], in_=ident[:, :], compare_op=ALU.not_equal, fill=1.0, base=0,
                            pattern=[[-1, P]], channel_multiplier=1).then_inc(id_done, 1)
            pool.wait_ge(consts, 1)
            pool.wait_ge(xms, 1)
            for b in range(HB):
                inv_root(rstd[:, b:b + 1], stat[:, 12 + b:13 + b], xrs)

            def join(n, a):
                pool.wait_ge(acc_step, KT * (n + 1))
                G.tensor_tensor(acc[:, a, 0], acc[:, a, 0], acc[:, a, 1], ALU.add).then_inc(joined, 1)

            def rope(n, half_count):
                pool.wait_ge(half_evac, half_count)
                x4 = qs[:].rearrange("p b (h d) -> p b h d", d=HD)
                t4 = rtmp[:].rearrange("p b (h d) -> p b h d", d=HD)
                for a, b in ((0, HALF), (HALF, 0)):
                    G.tensor_tensor(t4[:, :, :, a:a + HALF], x4[:, :, :, b:b + HALF],
                                    ropeS[:, :, a:a + HALF].unsqueeze(2).broadcast_to([P, HB, 8, HALF]),
                                    ALU.mult).then_inc(rope_b, 1)

            for c in range(4):
                for g in range(3 * c - 3, 3 * c - 1):
                    if c:
                        lo(g // 4, g % 4)
                join(2 * c, 0)
                if c:
                    lo((3 * c - 1) // 4, (3 * c - 1) % 4)
                join(2 * c + 1, 1)
            pool.wait_ge(tables, 1)
            for g in (9, 10, 11):
                lo(g // 4, g % 4)
            rope(0, 2)
            lo(3, 0)

            def normalise(i):
                for u in range(2):
                    pool.wait_ge(r_ready, 2 * i + u + 1)
                    G.tensor_tensor(s0[:, u], s0[:, u], den[:, u, 0].unsqueeze(2).broadcast_to([P, 4, P]),
                                    ALU.mult).then_inc(p_pool, 1)

            def attention(i, first, last):
                q = 3 + i
                if first:
                    pool.wait_ge(rope_c, 1)
                else:
                    pool.wait_ge(qk_pe, 3 * i)
                for twin in range(2):
                    G.tensor_copy(kst[:, :, :, twin], kr[:, :, bass.ds(2 * i * HD, 2 * HD)]
                                  .rearrange("p b (h d) -> p b h d", d=HD)).then_inc(k_staged, 1)
                rope(1 + i, 2 * (3 + i))
                lo(*after(q, 0))
                lo(*after(q, 1))
                join(8 + 2 * i, 0)
                lo(*after(q, 2))
                if first:
                    pool.wait_ge(half_evac, 4)
                else:
                    pool.wait_ge(pv_pe, 2 * i)
                G.tensor_copy(vst[:], vr[:, :, bass.ds(2 * i * HD, 2 * HD)]
                              .rearrange("p b (h d) -> p b h d", d=HD)).then_inc(v_staged, 1)
                if not last:
                    lo(*after(q, 3))
                join(9 + 2 * i, 1)
                normalise(i)

            attention(0, True, False)
            with pool.Fori(1, 3) as i:
                attention(i, False, False)
            attention(3, False, True)
            lo(7, 0)

            def diagonals(dst, rnd):
                for k in range(8):
                    ins = G.tensor_scalar(dst[:, k], ident[:, :], vcol[:, 8 * rnd + k:8 * rnd + k + 1], None,
                                          ALU.mult)
                ins.then_inc(diag_done, 1)

            with pool.Fori(0, 2) as i:
                for s in range(4):
                    lo(*after(7 + i, s))
                    if s % 2:
                        join(16 + 2 * i + s // 2, s // 2)
            pool.wait_ge(vc, 1)
            diagonals(diag1, 0)
            for s in range(2):
                lo(*after(9, s))
            pool.wait_ge(diag_pe, 2)
            diagonals(diag1, 1)
            for s in range(2, 4):
                lo(*after(9, s))
            for b in range(HB):
                pool.wait_ge(yms, 2 * b + 1)
                inv_root(rstd[:, b:b + 1], stat[:, 6 + b:7 + b], yrs)
                pool.wait_ge(yms, 2 * b + 2)
                inv_root(rstd[:, 2 + b:3 + b], stat[:, 8 + b:9 + b], yrs)

            def f1(i, with_mod):
                for u in range(2):
                    for s in range(4):
                        lo(*after(10 + 2 * i + u, s))
                        if with_mod and (u, s) == (1, 1):
                            join(GT_F - 1 + i, 0)

            f1(0, False)
            with pool.Fori(1, 5) as i:
                f1(i, True)
            with pool.Fori(5, FB - 1) as i:
                f1(i, False)
            for s in range(4):
                lo(*after(10 + 2 * (FB - 1), s))
            pool.wait_ge(vc, 2)
            diagonals(diag3, 0)
            for s in range(2):
                lo(*after(11 + 2 * (FB - 1), s))
            pool.wait_ge(diag_pe, 6)
            diagonals(diag3, 1)
            for s in range(2, 4):
                lo(*after(11 + 2 * (FB - 1), s))
            q2 = G_F2 // 4
            with pool.Fori(0, FT // 4 - 1) as i:
                for s in range(4):
                    lo(*after(q2 + i, s))
            for s in range(3):
                lo(*after(q2 + FT // 4 - 1, s))
            for b in range(HB):
                pool.wait_ge(y2ms, b + 1)
                inv_root(rstd[:, 4 + b:5 + b], stat[:, 10 + b:11 + b], y2rs)

        @block.tensor
        def _(pe):
            mm = nc.tensor.matmul

            def split_ready(q, s):
                for done in (hi_done, lo_done, lop_done):
                    pe.wait_ge(done, 4 * q + s + 1)

            def three(dst, hi, lo, s, n, start, stop):
                mm(dst, hi, whi[:, s % 2, n], start=start, stop=False)
                mm(dst, hi, wlo[:, s % 2, n], start=False, stop=False)
                return mm(dst, lo, whi[:, s % 2, n], start=False, stop=stop)

            def project(q, s, hT, lT, bank, half_sig, bank_free=None, slot=None):
                r = s if slot is None else slot
                split_ready(q, r)
                for b in range(HB):
                    if s == 0 and bank_free is not None:
                        pe.wait_ge(bank_free[0], bank_free[1] + b)
                    for t in range(WP):
                        k = WP * s + t
                        last = three(ps[:, bank + b], hT[:, k, b * P:(b + 1) * P], lT[:, k, b * P:(b + 1) * P],
                                     r, t, k == 0, k == KT - 1)
                    if s == 3 and b == 0:
                        last.then_inc(half_sig, 1)
                last.then_inc(pe_done, 1)

            def turn(dst, src):
                return nc.tensor.transpose(dst, src, ident[:, :])

            def reduce(n, a, bank=MCOL):
                pe.wait_ge(joined, n + 1)
                if not (isinstance(n, int) and n == 0):
                    pe.wait_ge(mod_added, n)
                for f in range(4):
                    last = mm(ps[:, bank, f:f + 1], acc[:, a, 0, f * P:(f + 1) * P], ones[:, 0:1],
                              start=True, stop=True)
                last.then_inc(reduced, 1)

            pe.wait_ge(id_done, 1)
            pe.wait_ge(consts, 1)
            for b in range(HB):
                pe.wait_ge(xn, b + 1)
                for r in range(4):
                    for t in range(4):
                        last = turn(ps[:, 4 * b + r, t * P:(t + 1) * P], x0[:, b, (4 * r + t) * P:(4 * r + t + 1) * P])
                    last.then_inc(xt, 1)
            pe.wait_ge(nT_done, 8)
            for c in range(4):
                reduce(2 * c, 0, MCOL0)
                reduce(2 * c + 1, 1, MCOL0)
                pe.wait_ge(h_ready, c + 1)
                for e in range(3):
                    g = 3 * c + e
                    project(g // 4, c, hThi, hTlo, 2 * e, half_done, slot=g % 4)

            def p_turned(i):
                for u in range(2):
                    pe.wait_ge(p_pool, 2 * i + u + 1)
                    for h in range(4):
                        t = turn(ps[:, 2 + u, h * P:(h + 1) * P], s0[:, u, h])
                    t.then_inc(pt_pe, 1)
                    pe.wait_ge(p_act, 2 * i + u + 1)
                    for part in range(2):
                        for h in range(4):
                            t = turn(ps[:, 4 + 2 * u + part, h * P:(h + 1) * P],
                                     s1[:, u, h, part * P:(part + 1) * P])
                        t.then_inc(pt_pe, 1)

            def outputs(i):
                pe.wait_ge(pt_act, 4 * i + 4)
                pe.wait_ge(pt_dve, 2 * i + 2)
                pe.wait_ge(v_staged, i + 1)
                for u in range(2):
                    for e in range(2):
                        o = ps[e * HD:(e + 1) * HD, 6 + u].rearrange("p (m b t) -> p m b t", m=2, b=HB)
                        heads = slice(2 * e, 2 * e + 2)
                        mm(o[:, :, 0], vst[:, 0, u], pT[:, u, 0, heads], start=True, stop=True)
                        mm(o[:, :, 1], vst[:, 0, u], pT[:, u, 1, heads], start=True, stop=False)
                        t = mm(o[:, :, 1], vst[:, 1, u], pT[:, u, 2, heads], start=False, stop=True)
                    t.then_inc(pv_pe, 1)

            def attention(i, first, last):
                q = 3 + i
                hT, lT = (oThi, oTlo) if last else (hThi, hTlo)

                def piece(s):
                    if last:
                        pe.wait_ge(oT_ready, 2 * s + 2)
                    project(q, s, hT, lT, 0, half_done, (half_evac, 2 * (3 + i) - 1))

                piece(0)
                if not first:
                    pe.wait_ge(mod_added, 7 + 2 * i)
                    p_turned(i - 1)
                piece(1)
                if not first:
                    pe.wait_ge(pt_act, 4 * i)
                    reduce(7 + 2 * i, 1)
                pe.wait_ge(rope_c, 2 + i)
                if not first:
                    pe.wait_ge(pt_dve, 2 * i)
                for pr in range(4):
                    for b in range(HB):
                        t = turn(ps[:, 2 + pr // 2, ((pr % 2) * 2 + b) * P:((pr % 2) * 2 + b + 1) * P],
                                 qr[:, b, pr * P:(pr + 1) * P])
                    if pr % 2:
                        t.then_inc(qk_pe, 1)
                pe.wait_ge(k_staged, 2 * i + 2)
                for u in range(2):
                    for b in range(HB):
                        t = turn(ps[:, 4, (2 * u + b) * P:(2 * u + b + 1) * P],
                                 kst[:, b, u].rearrange("p c d -> p (c d)"))
                t.then_inc(qk_pe, 1)
                if not first:
                    outputs(i - 1)
                pe.wait_ge(qT_done, 2 * i + 2)
                pe.wait_ge(kT_done, i + 1)
                pe.wait_ge(mod_added, 8 + 2 * i)
                for u in range(2):
                    if not first:
                        pe.wait_ge(oT_ready, 2 * (i - 1) + u + 1)
                    for e in range(2):
                        rows = slice(e * HD, (e + 1) * HD)
                        for m in range(2):
                            pr = 2 * u + m
                            mm(ps[:, 2 + e, (2 * u + m) * P:(2 * u + m + 1) * P], qT[rows, pr, 0:P],
                               kT[rows, u, 0:P], start=True, stop=True)
                            t = mm(ps[:, 4 + 2 * u + e, m * 192:(m + 1) * 192], qT[rows, pr, P:2 * P],
                                   kT[rows, u, CHUNK:], start=True, stop=True)
                t.then_inc(sc_pe, 1)
                piece(2)
                if last:
                    pe.wait_ge(sc_read, 4 * i + 4)
                    reduce(8 + 2 * i, 0)
                    pe.wait_ge(mod_added, 9 + 2 * i)
                    p_turned(i)
                    outputs(i)
                    pe.wait_ge(pt_act, 4 * i + 4)
                    reduce(9 + 2 * i, 1)
                piece(3)
                if not last:
                    pe.wait_ge(sc_read, 4 * i + 4)
                    reduce(8 + 2 * i, 0)

            attention(0, True, False)
            with pe.Fori(1, 3) as i:
                attention(i, False, False)
            attention(3, False, True)

            def spread(src, rnd, bank, n0):
                pe.wait_ge(diag_done, n0 // 2 + rnd + 1)
                for e in range(2):
                    for k in range(4):
                        t = mm(ps[:, bank + e, k * P:(k + 1) * P], ones[:, :], src[:, 4 * e + k],
                               start=True, stop=True)
                    t.then_inc(diag_pe, 1)

            with pe.Fori(1, 3) as w:
                for s in range(4):
                    project(6 + w, s, oThi, oTlo, 0, half_done, (half_evac, 2 * (6 + w) - 1))
                    if s == 2:
                        reduce(14 + 2 * w, 0)
                reduce(15 + 2 * w, 1)
            for s in range(4):
                project(9, s, oThi, oTlo, 0, half_done, (half_evac, 17))
                if s == 0:
                    spread(diag1, 0, 2, 0)
                if s == 2:
                    pe.wait_ge(grow_done, 2)
                    spread(diag1, 1, 2, 0)
            for b in range(HB):
                pe.wait_ge(n2_done, b + 1)
                for r in range(4):
                    n = 4 * b + r
                    if n >= 4 and H2_BANKS[n] in H2_BANKS[:n]:
                        pe.wait_ge(hf2, H2_BANKS.index(H2_BANKS[n]) + 1)
                    if n == 0:
                        pe.wait_ge(grow_done, 4)
                        pe.wait_ge(mod_added, 20)
                    for t in range(4):
                        last = turn(ps[:, H2_BANKS[n], t * P:(t + 1) * P], y[:, b, (4 * r + t) * P:(4 * r + t + 1) * P])
                    last.then_inc(n2_pe, 1)

            def gu_turn(i):
                for b in range(HB):
                    pe.wait_ge(gu_done, 2 * (i - 1) + b + 1)
                    for t in range(4):
                        last = turn(ps[:, 6 + b, t * P:(t + 1) * P], gu[:, b, t * P:(t + 1) * P])
                    last.then_inc(gu_pe, 1)

            def f1(i, first, with_mod, tail):
                q = 10 + 2 * i
                for s in range(4):
                    if first:
                        pe.wait_ge(h2_ready, 4 + s + 1)
                    free = (half_evac, 19) if first else (silu_done, 2 * i - 1)
                    project(q, s, hThi, hTlo, 0, f_half, free)
                    if s == 1 and not first:
                        gu_turn(i)
                for s in range(4):
                    project(q + 1, s, hThi, hTlo, 2, f_half, None if first else (gu_done, 2 * i - 1))
                    if with_mod and s == 2:
                        reduce(GT_F - 1 + i, 0)
                    if tail and s == 0:
                        spread(diag3, 0, 4, 4)
                    if tail and s == 2:
                        pe.wait_ge(grow_done, 6)
                        spread(diag3, 1, 4, 4)

            f1(0, True, False, False)
            with pe.Fori(1, 5) as i:
                f1(i, False, True, False)
            with pe.Fori(5, FB - 1) as i:
                f1(i, False, False, False)
            f1(FB - 1, False, False, True)
            gu_turn(FB)

            def f2(i, first, end):
                for s in range(4):
                    pe.wait_ge(gk_hi, 4 * i + s + 1)
                    pe.wait_ge(gk_lo, 4 * i + s + 1)
                    split_ready(G_F2 // 4 + i, s)
                    for b in range(HB):
                        tok = slice(b * P, (b + 1) * P)
                        for n in range(NB):
                            if first and s == 0 and b == 0 and n == 0:
                                pe.wait_ge(silu_done, 2 * FB)
                            if first and s == 0 and b == 0 and n == 2:
                                pe.wait_ge(gu_done, 2 * FB)
                            if first and s == 0 and b == 1 and n == 0:
                                pe.wait_ge(grow_done, 8)
                            if first and s == 0 and b == 1 and n == 2:
                                pe.wait_ge(guT_done, 2 * FB)
                            last = three(ps[:, 4 * b + n], hThi[:, s, tok], hTlo[:, s, tok], s, n,
                                         first and s == 0, end and s == 3)
                        if end and s == 3:
                            last.then_inc(y2_half, 1)
                    if not (end and s == 3):
                        last.then_inc(pe_done, 1)

            f2(0, True, False)
            with pe.Fori(1, FT // 4 - 1) as i:
                f2(i, False, False)
            f2(FT // 4 - 1, False, True)


SETUP_ANGLES = 17
F_MOD = [(0, 1), (2,), (3,), (4, 5), (6,), (7,), (), ()]
H2_BANKS = [2, 3, 4, 5, 6, 7, 2, 3]


def kernel(**inputs):
    import numpy as np
    import concourse.bacc as bacc
    from concourse import mybir as mb
    from concourse.bass_utils import run_bass_kernel_spmd as run

    def cols(a):
        return np.ascontiguousarray(a.reshape(-1, P).T)

    x = np.ascontiguousarray(inputs["x"])[0]
    gains = np.stack([cols(inputs["norm_g"][0, n]) for n in range(4)], axis=1)
    power = np.arange(0, HD, 2, dtype=np.float32) / np.float32(HD)
    invf = (np.float32(1.0) / np.power(np.float32(10000.0), power)).astype(np.float32)
    sinks = np.asarray(inputs["swa_sinks"])[0].reshape(4, 2, 2, 2).transpose(0, 1, 3, 2)
    sinks = np.repeat(sinks[:, :, None], HB, axis=2).reshape(1, 2 * QH)
    arrays = {
        "x": x,
        "cT": cols(inputs["c"][0]),
        "pos": np.ascontiguousarray(np.asarray(inputs["positions"])[0].reshape(HB, P).T),
        "invf": np.ascontiguousarray(np.broadcast_to(invf, (P, HALF))),
        "mod_w": np.ascontiguousarray(inputs["mod_w"][0]),
        "modbT": cols(inputs["mod_b"][0]),
        "gT": np.ascontiguousarray(gains),
        "w_qkv": np.ascontiguousarray(inputs["swa_w_qkv"][0]),
        "w_o": np.ascontiguousarray(inputs["swa_w_o"][0]),
        "sinks": np.ascontiguousarray(np.broadcast_to(sinks, (P, 2 * QH))),
        "w_in": np.ascontiguousarray(inputs["ffn_w_in"][0]),
        "w_out": np.ascontiguousarray(inputs["ffn_w_out"][0]),
    }
    nc = bacc.Bacc("TRN2", target_bir_lowering=False, num_devices=1)
    feed, args = {}, []
    for name, a in arrays.items():
        feed[f"in_{name}"] = a
        args.append(nc.dram_tensor(f"in_{name}", a.shape, mb.dt.from_np(a.dtype), kind="ExternalInput").ap())
    args.append(nc.dram_tensor("out_0", (T, D), mb.dt.float32, kind="ExternalOutput").ap())
    build(nc, *args)
    r = run(nc, [feed], core_ids=[0])
    return r.results[0]["out_0"].reshape(1, T, D)
```

```python
from contextlib import ExitStack

import concourse.bass as bass
from concourse import mybir

P = 128
F32 = mybir.dt.float32
F32R = mybir.dt.float32r
I32 = mybir.dt.int32
ACT = mybir.ActivationFunctionType
ALU = mybir.AluOpType
AX = mybir.AxisListType

D = 2048
T = 256
HB = T // P
KT = D // P
N = 512
NB = D // N
HD = 64
HALF = HD // 2
CHUNK = 64
QH = D // HD
KVH = 8
KVW = KVH * HD
F = 5632
FB = F // N
FT = F // P
SCALE = float(HD) ** -0.5
RMS_EPS = 1e-6
MASKED = -1e30
WP = 4
WRING = 4
SRING = 2
MP = 2
MPN = KT // MP
MRING = 4
G_KV, G_Q0, G_ATT, G_WO, G_F1 = 0, 8, 12, 28, 40
G_F2 = G_F1 + 2 * WP * FB
SH_M, SC_M, GT_M, SH_F, SC_F, GT_F = (NB * n for n in range(6))
PI_IN = 3.1415925
TWO_PI = (6.28125, 0.0019350051879882812, 3.0199188e-07)
ROUND = 12582912.0


def after(q, s, n=1):
    return q + (s + n) // 4, (s + n) % 4


def build(nc, x, cT, pos, invf, mod_w, modbT, gT, w_qkv, w_o, sinks, w_in, w_out, out):
    with ExitStack() as ctx:
        def sb(name, shape, dt=F32):
            return ctx.enter_context(nc.sbuf_tensor(name, shape, dt))

        def sem(name):
            return ctx.enter_context(nc.semaphore(name))

        raw = sb("raw", [P, WRING, WP, N])
        whi = sb("whi", [P, SRING, WP, N], F32R)
        wlo = sb("wlo", [P, SRING, WP, N], F32R)
        mraw = sb("mraw", [P, MRING, MP, N])
        acc = sb("acc", [P, 2, 2, N])
        hThi = sb("hThi", [P, KT, T], F32R)
        hTlo = sb("hTlo", [P, KT, T], F32R)
        ident = sb("ident", [P, P])
        ones = sb("ones", [P, P])
        ccol = sb("ccol", [P, KT])
        gcol = sb("gcol", [P, 4, KT])
        mbias = sb("mbias", [P, 6 * KT])
        modT = sb("modT", [P, 6 * KT])
        acol = sb("acol", [P, KT])
        vcol = sb("vcol", [P, KT])
        ropeC = sb("ropeC", [P, HB, HD])
        ropeS = sb("ropeS", [P, HB, HD])
        mask = sb("mask", [P, 3 * CHUNK])
        sinkp = sb("sinkp", [P, 2 * QH])
        sinkn = sb("sinkn", [P, 2 * QH])
        ssq = sb("ssq", [P, HB, NB])
        stat = sb("stat", [P, 16])
        rstd = sb("rstd", [P, 8])
        mhalf = sb("mhalf", [P, 1])
        kst = sb("kst", [P, HB, 2, 2, HD])
        vst = sb("vst", [P, HB, 2, HD])
        negm = sb("negm", [P, 2, HB, 4])
        esink = sb("esink", [P, 2, HB, 4])
        mx = sb("mx", [P, 2, HB, 4])
        den = sb("den", [P, 2, HB, 4])

        base = (nc.sbuf_base + 31) // 32 * 32
        ctx.enter_context(nc.sbuf_tensor("arena", [P, 80 * 256], F32))

        def at(name, kb, shape, dt=F32):
            return nc.alloc_sbuf_tensor_at(name, shape, dt, offset=base + int(kb * 1024))

        x0 = at("x0", 32, [P, HB, D])
        nT = at("nT", 48, [P, KT, T])
        posi = at("posi", 72, [P, HB], I32)
        posf = at("posf", 73, [P, HB])
        freq = at("freq", 74, [P, HALF])
        oThi = at("oThi", 0, [P, KT, T], F32R)
        oTlo = at("oTlo", 16, [P, KT, T], F32R)
        qs = at("qs", 32, [P, HB, N])
        qr = at("qr", 36, [P, HB, N])
        kr = at("kr", 40, [P, HB, KVW])
        qT = at("qT", 44, [P, 4, T])
        kT = at("kT", 48, [P, 2, T])
        s0 = at("s0", 50, [P, 2, 4, P])
        s1 = at("s1", 54, [P, 2, 4, 2 * P])
        pT = at("pT", 62, [P, 2, 3, 4, P])
        vr = at("vr", 74, [P, HB, KVW])
        rtmp = at("rtmp", 62, [P, HB, N])
        y = at("y", 32, [P, HB, D])
        x1 = at("x1", 48, [P, HB, D])
        grow = at("grow", 64, [P, D])
        diag1 = at("diag1", 72, [P, 8, P])
        junk = at("junk", 76, [P, N])
        hf = at("hf", 76, [P, 2, 4 * P])
        guT = at("guT", 0, [P, FT, T])
        diag3 = at("diag3", 44, [P, 8, P])
        sg = at("sg", 72, [P, HB, N])
        gu = at("gu", 76, [P, HB, N])

        ps = ctx.enter_context(nc.psum_tensor("ps", [P, 8, N], F32))

        w_loaded = [sem(f"w_loaded{s}") for s in range(WRING)]
        hi_done, lo_done, lop_done = sem("hi_done"), sem("lo_done"), sem("lop_done")
        pe_done = sem("pe_done")
        m_loaded = [sem(f"m_loaded{s}") for s in range(MRING)]
        acc_step = sem("acc_step")
        joined, reduced, mod_added = sem("joined"), sem("reduced"), sem("mod_added")
        c_in, k_in, x_in, x1_in = sem("c_in"), sem("k_in"), sem("x_in"), sem("x1_in")
        consts = sem("consts")
        id_zero, id_done = sem("id_zero"), sem("id_done")
        silu_c = sem("silu_c")
        setup = sem("setup")
        sines = sem("sines")
        tables = sem("tables")
        xsq, xms, xrs, xn, xt, nT_done = (sem(n) for n in ("xsq", "xms", "xrs", "xn", "xt", "nT_done"))
        a1, hf_done, hhi_done, h_ready = (sem(n) for n in ("a1", "hf_done", "hhi_done", "h_ready"))
        half_done, half_evac = sem("half_done"), sem("half_evac")
        rope_a, rope_b, rope_c = sem("rope_a"), sem("rope_b"), sem("rope_c")
        zeros, k_staged, v_staged = sem("zeros"), sem("k_staged"), sem("v_staged")
        qk_pe, qT_done, kT_done = sem("qk_pe"), sem("qT_done"), sem("kT_done")
        sc_pe, sc_read, rmax, m_ready, es_sum, es_done = (
            sem(n) for n in ("sc_pe", "sc_read", "rmax", "m_ready", "es_sum", "es_done"))
        p_exp, den_sum, r_ready, p_act, p_pool = (
            sem(n) for n in ("p_exp", "den_sum", "r_ready", "p_act", "p_pool"))
        pt_pe, pt_act = sem("pt_pe"), sem("pt_act")
        pv_pe, oThi_done, oT_ready = sem("pv_pe"), sem("oThi_done"), sem("oT_ready")
        vc, diag_done, diag_pe, grow_done = sem("vc"), sem("diag_done"), sem("diag_pe"), sem("grow_done")
        ysq, ychain, yms, yrs = sem("ysq"), sem("ychain"), sem("yms"), sem("yrs")
        x1_done, x1sq, n2_done, n2_pe = sem("x1_done"), sem("x1sq"), sem("n2_done"), sem("n2_pe")
        hf2, hhi2, h2_ready, a2 = sem("hf2"), sem("hhi2"), sem("h2_ready"), sem("a2")
        f_half, silu_done, gu_done, gu_pe, guT_done = (
            sem(n) for n in ("f_half", "silu_done", "gu_done", "gu_pe", "guT_done"))
        gk_hi, gk_lo = sem("gk_hi"), sem("gk_lo")
        y2_half, y2sq, y2ms, y2rs, y2_step, stored = (
            sem(n) for n in ("y2_half", "y2sq", "y2ms", "y2rs", "y2_step", "stored"))

        MCOL0, MCOL, MCOL2 = 6, 5, 7

        block = ctx.enter_context(nc.Block())

        @block.sync
        def _(sp):
            def load_w(q, s, src, first=False):
                if not first:
                    for done in (hi_done, lo_done, lop_done):
                        sp.wait_ge(done, 4 * q + s - 3)
                sp.dma_start(raw[:, s], src).then_inc(w_loaded[s], 16)

            def load_m(n, j, col=None, first=False):
                if not first:
                    sp.wait_ge(acc_step, MP * (MPN * n + j - 3))
                c = n if col is None else col
                src = mod_w.rearrange("(j t p) n -> j p t n", p=P, t=MP)[j][:, :, bass.ds(c * N, N)]
                sp.dma_start(mraw[:, j % 4], src).then_inc(m_loaded[j % 4], 16)

            def block_src(w, r, col):
                return w.rearrange("(r t p) n -> r p t n", p=P, t=WP)[r][:, :, bass.ds(col, N)]

            sp.dma_start(ccol[:, :], cT).then_inc(c_in, 16)
            def load_first_w(g):
                load_w(g // 4, g % 4, block_src(w_qkv, g // 3, (D, D + KVW, 0)[g % 3]), first=g < 4)

            for c in range(4):
                for u in range(2):
                    for j in range(MPN):
                        if (u, j) == (0, 2) and c:
                            load_first_w(3 * c - 1)
                        if (u, j) == (1, 4):
                            load_first_w(3 * c)
                        load_m(2 * c + u, j, (SH_M, SC_M)[u] + c, first=c == u == 0 and j < 4)
                load_first_w(3 * c + 1)
            for j in range(MPN):
                if j == 2:
                    load_first_w(11)
                if j == 4:
                    load_w(3, 0, block_src(w_qkv, 0, N))
                load_m(8, j)
            load_w(3, 1, block_src(w_qkv, 1, N))
            load_w(3, 2, block_src(w_qkv, 2, N))

            def beside(i, w, cols, n, last=False):
                for k in range(16):
                    if k == 7:
                        load_w(i, 3, block_src(w[0], 3, cols[0]))
                    if k == 12:
                        load_w(i + 1, 0, block_src(w[1], 0, cols[1]))
                    load_m(n + k // 8, k % 8)
                load_w(i + 1, 1, block_src(w[1], 1, cols[1]))
                if last:
                    for k in range(8):
                        load_m(n + 2, k)
                load_w(i + 1, 2, block_src(w[1], 2, cols[1]))

            with sp.Fori(0, 2) as i:
                beside(i + 3, (w_qkv, w_qkv), ((i + 1) * N, (i + 2) * N), 9 + 2 * i)
            beside(5, (w_qkv, w_o), (3 * N, 0), 13)
            beside(6, (w_o, w_o), (0, N), 15, last=True)
            with sp.Fori(1, 3) as i:
                for s in range(4):
                    q, r = (6 + i, 3) if s == 0 else (7 + i, s - 1)
                    load_w(q, r, block_src(w_o, r, i * N if s == 0 else (i + 1) * N))
                    for e in range(2):
                        load_m(17 + i, 2 * s + e)
            load_w(9, 3, block_src(w_o, 3, 3 * N))
            load_w(10, 0, block_src(w_in, 0, 0))
            sp.wait_ge(oT_ready, 8)
            for b in range(HB):
                sp.dma_start(x1[:, b], x[b * P:(b + 1) * P, :]).then_inc(x1_in, 16)
            for s in range(1, 4):
                load_w(10, s, block_src(w_in, s, 0))

            def f1_ahead(i, with_mod):
                for u in range(2):
                    for s in range(4):
                        col = F + i * N if u == 0 else (i + 1) * N
                        load_w(11 + 2 * i + u, s, block_src(w_in, s, col))
                        if with_mod:
                            for j in F_MOD[4 * u + s]:
                                load_m(GT_F - 1 + i, j)

            f1_ahead(0, False)
            with sp.Fori(1, 5) as i:
                f1_ahead(i, True)
            with sp.Fori(5, FB - 1) as i:
                f1_ahead(i, False)
            for s in range(4):
                load_w(11 + 2 * (FB - 1), s, block_src(w_in, s, F + (FB - 1) * N))
            with sp.Fori(0, FT // 4) as i:
                for s in range(4):
                    src = w_out.rearrange("(k s p) (a n) -> s p k a n", p=P, s=4, n=N)[s][:, bass.ds(i, 1)]
                    load_w(G_F2 // 4 + i, s, src)
            for b in range(HB):
                for e in range(2):
                    sp.wait_ge(y2_step, 6 * b + 4 + e + 1)
                    cs = slice(e * D // 2, (e + 1) * D // 2)
                    sp.dma_start(out[b * P:(b + 1) * P, cs], x1[:, b, cs]).then_inc(stored, 16)
            sp.wait_ge(stored, 16 * 2 * HB)

        @block.scalar
        def _(act):
            A = nc.scalar.activation

            def hi(q, s):
                act.wait_ge(w_loaded[s], 16 * (q + 1))
                if not (isinstance(q, int) and 4 * q + s < SRING):
                    act.wait_ge(pe_done, 4 * q + s - 1)
                A(whi[:, s % 2], raw[:, s], ACT.Copy).then_inc(hi_done, 1)

            for dst, src in ((posi, pos), (freq, invf), (gcol, gT), (mbias, modbT), (sinkp, sinks)):
                act.dma_start(dst[:], src).then_inc(k_in, 16)
            for b in range(HB):
                act.dma_start(x0[:, b], x[b * P:(b + 1) * P, :]).then_inc(x_in, 16)
            act.wait_ge(c_in, 16)
            A(ccol[:, :], ccol[:, :], ACT.Silu).then_inc(silu_c, 1)
            act.wait_ge(x_in, 32)
            for b in range(HB):
                A(nT[:, 8 * b:8 * b + 8].rearrange("p k t -> p (k t)"), x0[:, b], ACT.Square,
                  accum_out=ssq[:, b, 0:1]).then_inc(xsq, 1)
            for b in range(HB):
                act.wait_ge(xrs, b + 1)
                A(x0[:, b], x0[:, b], ACT.Copy, scale=rstd[:, b:b + 1]).then_inc(xn, 1)
            for b in range(HB):
                for r in range(4):
                    act.wait_ge(xt, 4 * b + r + 1)
                    A(nT[:, 4 * r:4 * r + 4, b * P:(b + 1) * P],
                      ps[:, 4 * b + r].rearrange("p (k t) -> p k t", t=P), ACT.Copy).then_inc(nT_done, 1)
            act.wait_ge(setup, 12)
            A(ropeC[:, :, 0:HALF], ropeC[:, :, 0:HALF], ACT.Sin).then_inc(sines, 1)
            A(ropeS[:, :, HALF:], ropeS[:, :, HALF:], ACT.Sin).then_inc(sines, 1)

            def half_ready(sig, count, q, b):
                if b == 0:
                    act.wait_ge(sig, count)
                else:
                    act.wait_ge(pe_done, 4 * q + 4)

            for c in range(4):
                act.wait_ge(hf_done, c + 1)
                A(hThi[:, 4 * c:4 * c + 4], nT[:, 4 * c:4 * c + 4], ACT.Copy).then_inc(hhi_done, 1)
                for g in range(3 * c, 3 * c + 3):
                    hi(g // 4, g % 4)
            for e, dst in enumerate((qs, vr, qs)):
                for b in range(HB):
                    act.wait_ge(half_done if b == 0 else pe_done, e + 1 if b == 0 else 10 + e)
                    if e == 2 and b == 0:
                        act.wait_ge(rope_c, 1)
                    A(dst[:, b], ps[:, 2 * e + b], ACT.Copy).then_inc(half_evac, 1)
                if e == 0:
                    hi(3, 0)

            def probs(i, u, between=None):
                act.wait_ge(m_ready, 2 * i + u + 1)
                for b in range(HB):
                    for h in range(4):
                        s = s0[:, u, h] if b == 0 else s1[:, u, h, CHUNK:]
                        p = A(s, s, ACT.Exp, bias=negm[:, u, b, h:h + 1], scale=SCALE,
                              accum_out=den[:, u, b, h:h + 1])
                    if b == 0 and between is not None:
                        between()
                p.then_inc(p_exp, 1)
                act.wait_ge(es_sum, 2 * i + u + 1)
                A(esink[:, u], esink[:, u], ACT.Exp).then_inc(es_done, 1)

            def normalise(i):
                act.wait_ge(r_ready, 2 * i + 2)
                for h in range(4):
                    s = s1[:, 1, h, CHUNK:]
                    p = A(s, s, ACT.Copy, scale=den[:, 1, 1, h:h + 1])
                p.then_inc(p_act, 1)

            def pT_out(i):
                for u in range(2):
                    for part in range(3):
                        act.wait_ge(pt_pe, 6 * i + 3 * u + part + 1)
                        A(pT[:, u, part].rearrange("p h t -> p (h t)"), ps[:, 3 + 2 * u + part if part else 2 + u],
                          ACT.Copy).then_inc(pt_act, 1)

            def oT_out(i):
                for u in range(2):
                    act.wait_ge(pv_pe, 2 * i + u + 1)
                    A(oThi[:, bass.ds(4 * i + 2 * u, 2)].rearrange("p a t -> p (a t)"), ps[:, 6 + u],
                      ACT.Copy).then_inc(oThi_done, 1)

            def attention(i, first, last):
                q = 3 + i
                hi(*after(q, 0))
                if not first:
                    normalise(i - 1)
                hi(*after(q, 1))
                if not first:
                    act.wait_ge(rope_c, i + 2)
                    pT_out(i - 1)
                hi(*after(q, 2))
                for e in range(2):
                    act.wait_ge(qk_pe, 3 * i + e + 1)
                    A(qT[:, 2 * e:2 * e + 2].rearrange("p a t -> p (a t)"), ps[:, 2 + e],
                      ACT.Copy).then_inc(qT_done, 1)
                act.wait_ge(qk_pe, 3 * i + 3)
                A(kT[:].rearrange("p u t -> p (u t)"), ps[:, 4], ACT.Copy).then_inc(kT_done, 1)
                if not first:
                    oT_out(i - 1)
                hi(*after(q, 3))
                probs(i, 0)
                if last:
                    probs(i, 1)
                    return

                def evac_q(b):
                    half_ready(half_done, i + 4, q, b)
                    A(qs[:, b], ps[:, b], ACT.Copy).then_inc(half_evac, 1)

                act.wait_ge(rope_c, i + 2)
                evac_q(0)
                probs(i, 1, between=lambda: evac_q(1))

            def evac_y(w):
                for b in range(HB):
                    half_ready(half_done, 7 + w, 6 + w, b)
                    if not (isinstance(w, int) and w == b == 0):
                        act.wait_ge(ysq, 2 * w + b)
                    A(junk[:, :], ps[:, b], ACT.Square, accum_out=ssq[:, b, bass.ds(w, 1)]).then_inc(ysq, 1)
                    A(y[:, b, bass.ds(w * N, N)], ps[:, b], ACT.Copy).then_inc(half_evac, 1)

            attention(0, True, False)
            with act.Fori(1, 3) as i:
                attention(i, False, False)
            attention(3, False, True)
            normalise(3)
            pT_out(3)
            oT_out(3)
            evac_y(0)

            def grow_evac(rnd, b0, n0):
                for e in range(2):
                    act.wait_ge(diag_pe, n0 + 2 * rnd + e + 1)
                    A(grow[:, (2 * rnd + e) * N:(2 * rnd + e + 1) * N], ps[:, b0 + e],
                      ACT.Copy).then_inc(grow_done, 1)

            with act.Fori(1, 3) as w:
                for s in range(4):
                    hi(*after(6 + w, s))
                evac_y(w)
            for s in range(4):
                hi(*after(9, s))
                if s == 0:
                    grow_evac(0, 2, 0)
                if s == 2:
                    grow_evac(1, 2, 0)
            evac_y(3)
            for b in range(HB):
                act.wait_ge(x1_done, b + 1)
                A(y[:, b], x1[:, b], ACT.Square, accum_out=stat[:, b:b + 1]).then_inc(x1sq, 1)
                act.wait_ge(yrs, 2 * b + 2)
                A(y[:, b], x1[:, b], ACT.Copy, scale=rstd[:, 2 + b:3 + b]).then_inc(n2_done, 1)
            for b in range(HB):
                for r in range(4):
                    act.wait_ge(hf2, 4 * b + r + 1)
                    A(hThi[:, 4 * r:4 * r + 4, b * P:(b + 1) * P],
                      hf[:, r % 2].rearrange("p (k t) -> p k t", t=P), ACT.Copy).then_inc(hhi2, 1)

            def f1(i, first, tail):
                q = 10 + 2 * i
                for u in range(2):
                    for s in range(4):
                        if tail and u == 1 and s == 3:
                            gk(0, 0)
                        hi(*after(q + u, s))
                        if u == 0 and s == 1 and not first:
                            act.wait_ge(gu_pe, 2 * i - 1)
                            A(guT[:, bass.ds(4 * i - 4, 4), 0:P],
                              ps[:, 6].rearrange("p (k t) -> p k t", t=P), ACT.Copy).then_inc(guT_done, 1)
                        if u == 0 and s == 3:
                            if not first:
                                act.wait_ge(gu_done, 2 * i)
                            for b in range(HB):
                                half_ready(f_half, 2 * i + 1, q, b)
                                A(sg[:, b], ps[:, b], ACT.Silu).then_inc(silu_done, 1)
                        if tail and u == 1 and s in (0, 2):
                            grow_evac(s // 2, 4, 4)

            def gk(i, s):
                act.wait_ge(pe_done, G_F2 + 4 * i + s - 3)
                if isinstance(i, int) and i == 0 and s == 0:
                    act.wait_ge(guT_done, 2 * (FB - 1))
                A(hThi[:, s], guT[:, bass.ds(4 * i + s, 1)].rearrange("p k t -> p (k t)"),
                  ACT.Copy).then_inc(gk_hi, 1)

            f1(0, True, False)
            with act.Fori(1, FB - 1) as i:
                f1(i, False, False)
            f1(FB - 1, False, True)
            act.wait_ge(gu_pe, 2 * FB - 1)
            A(guT[:, 4 * FB - 4:4 * FB, 0:P], ps[:, 6].rearrange("p (k t) -> p k t", t=P),
              ACT.Copy).then_inc(guT_done, 1)
            q2 = G_F2 // 4

            def f2(i, end=False):
                for s in range(4):
                    if s < 3:
                        gk(i, s + 1)
                        hi(*after(q2 + i, s))
                    elif not end:
                        gk(i + 1, 0)
                        hi(*after(q2 + i, s))

            f2(0)
            with act.Fori(1, FT // 4 - 1) as i:
                f2(i)
            act.wait_ge(guT_done, 2 * FB)
            f2(FT // 4 - 1, end=True)
            for b in range(HB):
                act.wait_ge(y2_half, b + 1)
                A(guT[:, 8 * b:8 * b + 8].rearrange("p k t -> p (k t)"),
                  ps[:, 4 * b:4 * b + 4].rearrange("p a n -> p (a n)"), ACT.Square,
                  accum_out=stat[:, 2 + b:3 + b]).then_inc(y2sq, 1)

        @block.vector
        def _(dve):
            V = nc.vector

            def lo(q, s):
                dve.wait_ge(hi_done, 4 * q + s + 1)
                V.tensor_tensor(wlo[:, s % 2, 0:2], raw[:, s, 0:2], whi[:, s % 2, 0:2].bitcast(F32),
                                ALU.subtract).then_inc(lo_done, 1)

            def mod(n, j, a, waits):
                dve.wait_ge(m_loaded[j % 4], 16 * (2 * n + j // 4 + 1))
                if j == 0 and waits is not None:
                    dve.wait_ge(reduced, waits)
                for t in range(MP):
                    k = MP * j + t
                    c = ccol[:, k:k + 1]
                    if k < 2:
                        ins = V.tensor_scalar(acc[:, a, t], mraw[:, j % 4, t], c, None, ALU.mult)
                    else:
                        dve.wait_ge(acc_step, KT * n + k - 1)
                        ins = V.scalar_tensor_tensor(acc[:, a, t], mraw[:, j % 4, t], c, acc[:, a, t],
                                                     ALU.mult, ALU.add)
                    ins.then_inc(acc_step, 1)

            def mod_add(n, bank=MCOL):
                dve.wait_ge(reduced, n + 1)
                V.tensor_tensor(modT[:, bass.ds(4 * n, 4)], ps[:, bank, 0:4], mbias[:, bass.ds(4 * n, 4)],
                                ALU.add).then_inc(mod_added, 1)

            count = [0]

            def link(ins):
                count[0] += 1
                ins.then_inc(setup, 1)
                dve.wait_ge(setup, count[0])

            V.memset(ones[:, :], 1.0)
            V.memset(mhalf[:, :], -0.5)
            V.memset(mask[0:CHUNK, 0:2 * CHUNK], 0.0)
            V.memset(mask[CHUNK:P, CHUNK:], 0.0)
            V.memset(mask[CHUNK:P, 0:CHUNK], MASKED)
            V.memset(mask[0:CHUNK, 2 * CHUNK:], MASKED).then_inc(consts, 1)
            dve.wait_ge(k_in, 80)
            link(V.tensor_copy(posf[:, :], posi[:, :]))
            link(V.tensor_tensor(ropeS[:, :, HALF:], posf[:, :].unsqueeze(2).broadcast_to([P, HB, HALF]),
                                 freq[:, :].unsqueeze(1).broadcast_to([P, HB, HALF]), ALU.mult))
            link(V.tensor_scalar(sinkn[:, :], sinkp[:, :], -1.0, None, ALU.mult))
            turns = ropeC[:, :, HALF:]
            ang, angc = ropeS[:, :, HALF:], ropeC[:, :, 0:HALF]
            link(V.tensor_scalar(angc, ang, 0.0, None, ALU.add))
            for r, shift in ((ang, 0.0), (angc, 0.25)):
                link(V.tensor_scalar(turns, r, 1.0 / (2.0 * 3.141592653589793), shift, ALU.mult, ALU.add))
                link(V.tensor_scalar(turns, turns, ROUND, -ROUND, ALU.add, ALU.add))
                for part in TWO_PI:
                    link(V.scalar_tensor_tensor(r, turns, -part, r, ALU.mult, ALU.add))
            link(V.tensor_scalar(angc, angc, 1.5707963267948966, PI_IN, ALU.add, ALU.min))
            link(V.tensor_scalar(angc, angc, -PI_IN, None, ALU.max))
            link(V.tensor_scalar(ang, ang, PI_IN, -PI_IN, ALU.min, ALU.max))
            assert count[0] == SETUP_ANGLES
            dve.wait_ge(xsq, 2)
            V.tensor_scalar(stat[:, 12:14], ssq[:, :, 0], 1.0 / D, RMS_EPS, ALU.mult, ALU.add).then_inc(xms, 1)
            dve.wait_ge(silu_c, 1)
            def first_mod(n, js):
                for j in js:
                    mod(n, j, n % 2, n - 1 if n >= 2 else None)

            def modulate(c):
                ks = slice(4 * c, 4 * c + 4)
                dve.wait_ge(reduced, 2 * c + 2)
                V.tensor_tensor(modT[:, 0:2 * KT].rearrange("p (s k) -> p s k", s=2)[:, :, ks],
                                ps[:, MCOL0, 0:8].rearrange("p (s k) -> p s k", s=2),
                                mbias[:, 0:2 * KT].rearrange("p (s k) -> p s k", s=2)[:, :, ks],
                                ALU.add).then_inc(mod_added, 2)
                dve.wait_ge(mod_added, 2 * c + 2)
                V.scalar_tensor_tensor(acol[:, ks], modT[:, KT + 4 * c:KT + 4 * c + 4], 1.0, gcol[:, 0, ks],
                                       ALU.add, ALU.mult).then_inc(a1, 1)
                dve.wait_ge(a1, c + 1)
                for k in range(4 * c, 4 * c + 4):
                    ins = V.tensor_scalar(nT[:, k], nT[:, k], acol[:, k:k + 1], modT[:, k:k + 1],
                                          ALU.mult, ALU.add)
                ins.then_inc(hf_done, 1)

            def h_lo(c):
                dve.wait_ge(hhi_done, c + 1)
                V.tensor_tensor(hTlo[:, 4 * c:4 * c + 4], nT[:, 4 * c:4 * c + 4],
                                hThi[:, 4 * c:4 * c + 4].bitcast(F32), ALU.subtract).then_inc(h_ready, 1)

            def rope_parts(n, half_count, dst):
                dve.wait_ge(half_evac, half_count)
                V.tensor_tensor(dst.rearrange("p b (h d) -> p b h d", d=HD),
                                qs[:].rearrange("p b (h d) -> p b h d", d=HD),
                                ropeC[:].unsqueeze(2).broadcast_to([P, HB, 8, HD]), ALU.mult).then_inc(rope_a, 1)
                yield
                dve.wait_ge(rope_a, n + 1)
                dve.wait_ge(rope_b, 2 * n + 2)
                V.tensor_tensor(dst, dst, rtmp[:], ALU.add).then_inc(rope_c, 1)
                yield

            for c in range(4):
                first_mod(2 * c, range(0, 4))
                if c == 0:
                    dve.wait_ge(sines, 2)
                    V.tensor_copy(ropeC[:, :, HALF:], ropeC[:, :, 0:HALF])
                    V.tensor_scalar(ropeS[:, :, 0:HALF], ropeS[:, :, HALF:], -1.0, None,
                                    ALU.mult).then_inc(tables, 1)
                    dve.wait_ge(nT_done, 8)
                else:
                    modulate(c - 1)
                first_mod(2 * c, range(4, 8))
                if c:
                    h_lo(c - 1)
                    for g in (3 * c - 3, 3 * c - 2):
                        lo(g // 4, g % 4)
                first_mod(2 * c + 1, range(0, 4))
                if c:
                    lo((3 * c - 1) // 4, (3 * c - 1) % 4)
                first_mod(2 * c + 1, range(4, 8))
            first_mod(8, range(0, 2))
            modulate(3)
            first_mod(8, range(2, 3))
            h_lo(3)
            lo(2, 1)
            lo(2, 2)
            dve.wait_ge(h_ready, 4)
            V.memset(s1[:, :, :, 0:CHUNK], 0.0).then_inc(zeros, 1)
            first_mod(8, range(3, 5))
            lo(2, 3)
            keys = rope_parts(0, 2, kr[:])
            next(keys)
            first_mod(8, range(5, 8))
            next(keys)
            lo(3, 0)

            def max_and_sinks(i):
                def second(u):
                    V.tensor_tensor(s1[:, u, :, CHUNK:].rearrange("p (e m) k -> p e m k", e=2),
                                    ps[:, 4 + 2 * u:6 + 2 * u, 0:6 * CHUNK].rearrange("p e (m k) -> p e m k", m=2),
                                    mask[:].unsqueeze(1).unsqueeze(1).broadcast_to([P, 2, 2, 3 * CHUNK]),
                                    ALU.add).then_inc(sc_read, 1)

                def first_half(u):
                    V.tensor_tensor(s0[:, u].rearrange("p (e m) k -> p e m k", e=2),
                                    ps[:, 2:4, u * 256:(u + 1) * 256].rearrange("p e (m k) -> p e m k", m=2),
                                    mask[:, CHUNK:].unsqueeze(1).unsqueeze(1).broadcast_to([P, 2, 2, P]),
                                    ALU.add).then_inc(sc_read, 1)

                dve.wait_ge(sc_pe, 2 * i + 1)
                second(0)
                dve.wait_ge(sc_pe, 2 * i + 2)
                first_half(0)
                second(1)
                first_half(1)
                for u in range(2):
                    dve.wait_ge(sc_read, 4 * i + 2 * u + 2)
                    V.tensor_reduce(mx[:, u, 0], s0[:, u], AX.X, ALU.max).then_inc(rmax, 1)
                    V.tensor_reduce(mx[:, u, 1], s1[:, u, :, CHUNK:], AX.X, ALU.max).then_inc(rmax, 1)
                    dve.wait_ge(rmax, 4 * i + 2 * u + 2)
                    V.scalar_tensor_tensor(negm[:, u].rearrange("p b h -> p (b h)"),
                                           mx[:, u].rearrange("p b h -> p (b h)"), -SCALE,
                                           sinkn[:, bass.ds(16 * i + 8 * u, 8)], ALU.mult,
                                           ALU.min).then_inc(m_ready, 1)
                    dve.wait_ge(m_ready, 2 * i + u + 1)
                    V.tensor_tensor(esink[:, u].rearrange("p b h -> p (b h)"),
                                    negm[:, u].rearrange("p b h -> p (b h)"),
                                    sinkp[:, bass.ds(16 * i + 8 * u, 8)], ALU.add).then_inc(es_sum, 1)

            def denominator(i, u):
                dve.wait_ge(p_exp, 2 * i + u + 1)
                dve.wait_ge(es_done, 2 * i + u + 1)
                V.tensor_tensor(den[:, u], den[:, u], esink[:, u], ALU.add).then_inc(den_sum, 1)
                dve.wait_ge(den_sum, 2 * i + u + 1)
                V.reciprocal(den[:, u], den[:, u]).then_inc(r_ready, 1)

            def oT_lo(i):
                for u in range(2):
                    dve.wait_ge(oThi_done, 2 * i + u + 1)
                    V.tensor_tensor(oTlo[:, bass.ds(4 * i + 2 * u, 2)].rearrange("p a t -> p (a t)"), ps[:, 6 + u],
                                    oThi[:, bass.ds(4 * i + 2 * u, 2)].rearrange("p a t -> p (a t)").bitcast(F32),
                                    ALU.subtract).then_inc(oT_ready, 1)

            def attention(i, first, last):
                q = 3 + i
                m1, m2 = 9 + 2 * i, 10 + 2 * i

                def m(which, *js):
                    for j in js:
                        n = m1 - 1 + which
                        mod(n, j, which % 2, n - 1)

                turned = rope_parts(1 + i, 2 * (3 + i), qr[:])
                next(turned)
                if not first:
                    denominator(i - 1, 1)
                lo(*after(q, 0))
                if first:
                    mod_add(8, MCOL0)
                next(turned)
                m(1, 0, 1)
                if not first:
                    mod_add(8 + 2 * i, MCOL2)
                m(1, 2, 3, 4)
                lo(*after(q, 1))
                m(1, 5, 6, 7)
                lo(*after(q, 2))
                m(2, 0)
                if not first:
                    oT_lo(i - 1)
                mod_add(m1)
                m(2, 1, 2, 3)
                max_and_sinks(i)
                lo(*after(q, 3))
                m(2, 4)
                denominator(i, 0)
                m(2, 5)
                if last:
                    denominator(i, 1)
                m(2, 6, 7)

            attention(0, True, False)
            with dve.Fori(1, 3) as i:
                attention(i, False, False)
            attention(3, False, True)
            for j in range(4):
                mod(17, j, 1, 16)
            oT_lo(3)
            mod_add(16)
            for j in range(4, 8):
                mod(17, j, 1, 16)

            V.tensor_tensor(vcol[:, :], modT[:, 2 * KT:3 * KT], gcol[:, 1], ALU.mult).then_inc(vc, 1)
            with dve.Fori(1, 3) as w:
                for s, js in enumerate(((0, 1), (2, 3, 4), (5, 6, 7), ())):
                    lo(*after(6 + w, s))
                    if s == 0:
                        mod_add(16 + w)
                    for j in js:
                        mod(17 + w, j, 0, 17 + w)
            mod_add(19)
            dve.wait_ge(mod_added, 20)
            V.scalar_tensor_tensor(acol[:, :], modT[:, 4 * KT:5 * KT], 1.0, gcol[:, 2], ALU.add,
                                   ALU.mult).then_inc(a2, 1)
            for s in range(4):
                lo(*after(9, s))
            dve.wait_ge(grow_done, 4)
            dve.wait_ge(x1_in, 32)
            for b in range(HB):
                dve.wait_ge(ysq, 7 + b)
                V.tensor_reduce(stat[:, 4 + b:5 + b], ssq[:, b], AX.X, ALU.add).then_inc(ychain, 1)
                dve.wait_ge(ychain, 2 * b + 1)
                V.tensor_scalar(stat[:, 6 + b:7 + b], stat[:, 4 + b:5 + b], 1.0 / D, RMS_EPS, ALU.mult,
                                ALU.add).then_inc(yms, 1)
                dve.wait_ge(half_evac, 19 + b)
                dve.wait_ge(yrs, 2 * b + 1)
                V.scalar_tensor_tensor(y[:, b], y[:, b], rstd[:, b:b + 1], grow[:, :], ALU.mult,
                                       ALU.mult).then_inc(ychain, 1)
                dve.wait_ge(ychain, 2 * b + 2)
                V.tensor_tensor(x1[:, b], x1[:, b], y[:, b], ALU.add).then_inc(x1_done, 1)
                dve.wait_ge(x1sq, b + 1)
                V.tensor_scalar(stat[:, 8 + b:9 + b], stat[:, b:b + 1], 1.0 / D, RMS_EPS, ALU.mult,
                                ALU.add).then_inc(yms, 1)
            dve.wait_ge(a2, 1)

            def h2_mod(b, r):
                dve.wait_ge(n2_pe, 4 * b + r + 1)
                if 4 * b + r >= 2:
                    dve.wait_ge(h2_ready, 4 * b + r - 1)
                bank = H2_BANKS[4 * b + r]
                for t in range(4):
                    k = 4 * r + t
                    ins = V.tensor_scalar(hf[:, r % 2, t * P:(t + 1) * P], ps[:, bank, t * P:(t + 1) * P],
                                          acol[:, k:k + 1], modT[:, 3 * KT + k:3 * KT + k + 1], ALU.mult, ALU.add)
                ins.then_inc(hf2, 1)

            def h2_lo(b, r):
                dve.wait_ge(hhi2, 4 * b + r + 1)
                V.tensor_tensor(hTlo[:, 4 * r:4 * r + 4, b * P:(b + 1) * P],
                                hf[:, r % 2].rearrange("p (k t) -> p k t", t=P),
                                hThi[:, 4 * r:4 * r + 4, b * P:(b + 1) * P].bitcast(F32),
                                ALU.subtract).then_inc(h2_ready, 1)

            steps = [(b, r) for b in range(HB) for r in range(4)]
            h2_mod(*steps[0])
            for n in range(1, 8):
                h2_mod(*steps[n])
                h2_lo(*steps[n - 1])
            h2_lo(*steps[7])

            def f1(i, first, with_mod, tail):
                q = 10 + 2 * i
                for u in range(2):
                    for s in range(4):
                        if tail and u == 1 and s == 3:
                            gk_low(0, 0)
                        lo(*after(q + u, s))
                        if u == 0 and s == 1 and not first:
                            dve.wait_ge(gu_pe, 2 * i)
                            V.tensor_copy(guT[:, bass.ds(4 * i - 4, 4), P:2 * P],
                                          ps[:, 7].rearrange("p (k t) -> p k t", t=P)).then_inc(guT_done, 1)
                        if with_mod:
                            for j in F_MOD[4 * u + s]:
                                mod(GT_F - 1 + i, j, 0, GT_F - 1 + i)
                if with_mod:
                    mod_add(GT_F - 1 + i)
                for b in range(HB):
                    if b == 0:
                        dve.wait_ge(f_half, 2 * i + 2)
                    else:
                        dve.wait_ge(pe_done, 4 * (q + 1) + 4)
                    dve.wait_ge(silu_done, 2 * i + b + 1)
                    V.tensor_tensor(gu[:, b], sg[:, b], ps[:, 2 + b], ALU.mult).then_inc(gu_done, 1)

            def gk_low(i, s):
                dve.wait_ge(gk_hi, 4 * i + s + 1)
                V.tensor_tensor(hTlo[:, s], guT[:, bass.ds(4 * i + s, 1)].rearrange("p k t -> p (k t)"),
                                hThi[:, s].bitcast(F32), ALU.subtract).then_inc(gk_lo, 1)

            f1(0, True, False, False)
            with dve.Fori(1, 5) as i:
                f1(i, False, True, False)
            dve.wait_ge(mod_added, 24)
            dve.wait_ge(diag_done, 2)
            V.tensor_tensor(vcol[:, :], modT[:, 5 * KT:6 * KT], gcol[:, 3], ALU.mult).then_inc(vc, 1)
            with dve.Fori(5, FB - 1) as i:
                f1(i, False, False, False)
            f1(FB - 1, False, False, True)
            dve.wait_ge(gu_pe, 2 * FB)
            V.tensor_copy(guT[:, 4 * FB - 4:4 * FB, P:2 * P],
                          ps[:, 7].rearrange("p (k t) -> p k t", t=P)).then_inc(guT_done, 1)
            q2 = G_F2 // 4

            def f2(i, end=False):
                for s in range(4):
                    if s < 3:
                        gk_low(i, s + 1)
                        lo(*after(q2 + i, s))
                    elif not end:
                        gk_low(i + 1, 0)
                        lo(*after(q2 + i, s))

            f2(0)
            with dve.Fori(1, FT // 4 - 1) as i:
                f2(i)
            f2(FT // 4 - 1, end=True)
            for b in range(HB):
                dve.wait_ge(y2sq, b + 1)
                V.tensor_scalar(stat[:, 10 + b:11 + b], stat[:, 2 + b:3 + b], 1.0 / D, RMS_EPS, ALU.mult,
                                ALU.add).then_inc(y2ms, 1)
                dve.wait_ge(y2rs, b + 1)
                for e in range(4):
                    cs = slice(e * N, (e + 1) * N)
                    V.scalar_tensor_tensor(guT[:, 16 + 2 * e:18 + 2 * e].rearrange("p k t -> p (k t)"),
                                           ps[:, 4 * b + e], rstd[:, 4 + b:5 + b], grow[:, cs], ALU.mult,
                                           ALU.mult).then_inc(y2_step, 1)
                for e in range(2):
                    cs = slice(e * D // 2, (e + 1) * D // 2)
                    dve.wait_ge(y2_step, 6 * b + 2 * e + 2)
                    V.tensor_tensor(x1[:, b, cs], x1[:, b, cs],
                                    guT[:, 16 + 4 * e:20 + 4 * e].rearrange("p k t -> p (k t)"),
                                    ALU.add).then_inc(y2_step, 1)

        @block.gpsimd
        def _(pool):
            G = nc.gpsimd

            def lo(q, s):
                pool.wait_ge(hi_done, 4 * q + s + 1)
                G.tensor_tensor(wlo[:, s % 2, 2:4], raw[:, s, 2:4], whi[:, s % 2, 2:4].bitcast(F32),
                                ALU.subtract).then_inc(lop_done, 1)

            def inv_root(dst, src, done):
                G.tensor_tensor(dst, src, mhalf[:, :], ALU.pow).then_inc(done, 1)

            G.memset(ident[:, :], 0.0).then_inc(id_zero, 1)
            pool.wait_ge(id_zero, 1)
            G.affine_select(out=ident[:, :], in_=ident[:, :], compare_op=ALU.not_equal, fill=1.0, base=0,
                            pattern=[[-1, P]], channel_multiplier=1).then_inc(id_done, 1)
            pool.wait_ge(consts, 1)
            pool.wait_ge(xms, 1)
            for b in range(HB):
                inv_root(rstd[:, b:b + 1], stat[:, 12 + b:13 + b], xrs)

            def join(n, a):
                pool.wait_ge(acc_step, KT * (n + 1))
                G.tensor_tensor(acc[:, a, 0], acc[:, a, 0], acc[:, a, 1], ALU.add).then_inc(joined, 1)

            def rope(n, half_count):
                pool.wait_ge(half_evac, half_count)
                x4 = qs[:].rearrange("p b (h d) -> p b h d", d=HD)
                t4 = rtmp[:].rearrange("p b (h d) -> p b h d", d=HD)
                for a, b in ((0, HALF), (HALF, 0)):
                    G.tensor_tensor(t4[:, :, :, a:a + HALF], x4[:, :, :, b:b + HALF],
                                    ropeS[:, :, a:a + HALF].unsqueeze(2).broadcast_to([P, HB, 8, HALF]),
                                    ALU.mult).then_inc(rope_b, 1)

            for c in range(4):
                for g in range(3 * c - 3, 3 * c - 1):
                    if c:
                        lo(g // 4, g % 4)
                join(2 * c, 0)
                if c:
                    lo((3 * c - 1) // 4, (3 * c - 1) % 4)
                join(2 * c + 1, 1)
            pool.wait_ge(tables, 1)
            for g in (9, 10, 11):
                lo(g // 4, g % 4)
            rope(0, 2)
            join(8, 0)
            lo(3, 0)

            def normalise(i, u):
                pool.wait_ge(r_ready, 2 * i + u + 1)
                G.tensor_tensor(s0[:, u], s0[:, u], den[:, u, 0].unsqueeze(2).broadcast_to([P, 4, P]),
                                ALU.mult).then_inc(p_pool, 1)
                if u == 0:
                    p = s1[:, u, :, CHUNK:]
                    G.tensor_tensor(p, p, den[:, u, 1].unsqueeze(2).broadcast_to([P, 4, 3 * CHUNK]),
                                    ALU.mult).then_inc(p_pool, 1)

            def attention(i, first, last):
                q = 3 + i
                rope(1 + i, 2 * (3 + i))
                if not first:
                    normalise(i - 1, 1)
                lo(*after(q, 0))
                lo(*after(q, 1))
                if first:
                    pool.wait_ge(rope_c, 1)
                else:
                    pool.wait_ge(qk_pe, 3 * i)
                for twin in range(2):
                    G.tensor_copy(kst[:, :, :, twin], kr[:, :, bass.ds(2 * i * HD, 2 * HD)]
                                  .rearrange("p b (h d) -> p b h d", d=HD)).then_inc(k_staged, 1)
                join(9 + 2 * i, 1)
                lo(*after(q, 2))
                if first:
                    pool.wait_ge(half_evac, 4)
                else:
                    pool.wait_ge(pv_pe, 2 * i)
                G.tensor_copy(vst[:], vr[:, :, bass.ds(2 * i * HD, 2 * HD)]
                              .rearrange("p b (h d) -> p b h d", d=HD)).then_inc(v_staged, 1)
                lo(*after(q, 3))
                normalise(i, 0)
                if last:
                    normalise(i, 1)
                join(10 + 2 * i, 0)

            attention(0, True, False)
            with pool.Fori(1, 3) as i:
                attention(i, False, False)
            attention(3, False, True)
            join(17, 1)

            def diagonals(dst, rnd):
                for k in range(8):
                    ins = G.tensor_scalar(dst[:, k], ident[:, :], vcol[:, 8 * rnd + k:8 * rnd + k + 1], None,
                                          ALU.mult)
                ins.then_inc(diag_done, 1)

            with pool.Fori(1, 3) as w:
                for s in range(4):
                    lo(*after(6 + w, s))
                    if s == 2:
                        join(17 + w, 0)
            pool.wait_ge(vc, 1)
            diagonals(diag1, 0)
            for s in range(2):
                lo(*after(9, s))
            pool.wait_ge(diag_pe, 2)
            diagonals(diag1, 1)
            for s in range(2, 4):
                lo(*after(9, s))
            for b in range(HB):
                pool.wait_ge(yms, 2 * b + 1)
                inv_root(rstd[:, b:b + 1], stat[:, 6 + b:7 + b], yrs)
                pool.wait_ge(yms, 2 * b + 2)
                inv_root(rstd[:, 2 + b:3 + b], stat[:, 8 + b:9 + b], yrs)

            def f1(i, with_mod):
                for u in range(2):
                    for s in range(4):
                        lo(*after(10 + 2 * i + u, s))
                        if with_mod and (u, s) == (1, 1):
                            join(GT_F - 1 + i, 0)

            f1(0, False)
            with pool.Fori(1, 5) as i:
                f1(i, True)
            with pool.Fori(5, FB - 1) as i:
                f1(i, False)
            for s in range(4):
                lo(*after(10 + 2 * (FB - 1), s))
            pool.wait_ge(vc, 2)
            diagonals(diag3, 0)
            for s in range(2):
                lo(*after(11 + 2 * (FB - 1), s))
            pool.wait_ge(diag_pe, 6)
            diagonals(diag3, 1)
            for s in range(2, 4):
                lo(*after(11 + 2 * (FB - 1), s))
            q2 = G_F2 // 4
            with pool.Fori(0, FT // 4 - 1) as i:
                for s in range(4):
                    lo(*after(q2 + i, s))
            for s in range(3):
                lo(*after(q2 + FT // 4 - 1, s))
            for b in range(HB):
                pool.wait_ge(y2ms, b + 1)
                inv_root(rstd[:, 4 + b:5 + b], stat[:, 10 + b:11 + b], y2rs)

        @block.tensor
        def _(pe):
            mm = nc.tensor.matmul

            def split_ready(q, s):
                for done in (hi_done, lo_done, lop_done):
                    pe.wait_ge(done, 4 * q + s + 1)

            def three(dst, hi, lo, s, n, start, stop):
                mm(dst, hi, whi[:, s % 2, n], start=start, stop=False)
                mm(dst, hi, wlo[:, s % 2, n], start=False, stop=False)
                return mm(dst, lo, whi[:, s % 2, n], start=False, stop=stop)

            def project(q, s, hT, lT, bank, half_sig, bank_free=None, slot=None, halves=(0, 1)):
                r = s if slot is None else slot
                split_ready(q, r)
                for b in halves:
                    if s == 0 and bank_free is not None:
                        pe.wait_ge(bank_free[0], bank_free[1] + b)
                    for t in range(WP):
                        k = WP * s + t
                        last = three(ps[:, bank + b], hT[:, k, b * P:(b + 1) * P], lT[:, k, b * P:(b + 1) * P],
                                     r, t, k == 0, k == KT - 1)
                    if s == 3 and b == 0:
                        last.then_inc(half_sig, 1)
                if 1 in halves:
                    last.then_inc(pe_done, 1)

            def turn(dst, src):
                return nc.tensor.transpose(dst, src, ident[:, :])

            def reduce(n, a, bank=MCOL, col=0):
                pe.wait_ge(joined, n + 1)
                if not (col or isinstance(n, int) and n == 0):
                    pe.wait_ge(mod_added, n)
                for f in range(4):
                    last = mm(ps[:, bank, col + f:col + f + 1], acc[:, a, 0, f * P:(f + 1) * P], ones[:, 0:1],
                              start=True, stop=True)
                last.then_inc(reduced, 1)

            pe.wait_ge(id_done, 1)
            pe.wait_ge(consts, 1)
            for b in range(HB):
                pe.wait_ge(xn, b + 1)
                for r in range(4):
                    for t in range(4):
                        last = turn(ps[:, 4 * b + r, t * P:(t + 1) * P], x0[:, b, (4 * r + t) * P:(4 * r + t + 1) * P])
                    last.then_inc(xt, 1)
            pe.wait_ge(nT_done, 8)
            for c in range(4):
                reduce(2 * c, 0, MCOL0)
                reduce(2 * c + 1, 1, MCOL0, 4)
                pe.wait_ge(h_ready, c + 1)
                for e in range(3):
                    g = 3 * c + e
                    project(g // 4, c, hThi, hTlo, 2 * e, half_done, slot=g % 4)
            reduce(8, 0, MCOL0)

            def p_turned(i, added):
                for u in range(2):
                    pe.wait_ge(p_pool, 3 * i + 2 * u + 1)
                    for h in range(4):
                        t = turn(ps[:, 2 + u, h * P:(h + 1) * P], s0[:, u, h])
                    t.then_inc(pt_pe, 1)
                    if u == 0:
                        pe.wait_ge(p_pool, 3 * i + 2)
                    else:
                        pe.wait_ge(p_act, i + 1)
                    for part in range(2):
                        if u == part == 1:
                            pe.wait_ge(mod_added, added)
                        for h in range(4):
                            t = turn(ps[:, 4 + 2 * u + part, h * P:(h + 1) * P],
                                     s1[:, u, h, part * P:(part + 1) * P])
                        t.then_inc(pt_pe, 1)

            def outputs(i):
                pe.wait_ge(pt_act, 6 * i + 6)
                pe.wait_ge(v_staged, i + 1)
                for u in range(2):
                    for e in range(2):
                        o = ps[e * HD:(e + 1) * HD, 6 + u].rearrange("p (m b t) -> p m b t", m=2, b=HB)
                        heads = slice(2 * e, 2 * e + 2)
                        mm(o[:, :, 0], vst[:, 0, u], pT[:, u, 0, heads], start=True, stop=True)
                        mm(o[:, :, 1], vst[:, 0, u], pT[:, u, 1, heads], start=True, stop=False)
                        t = mm(o[:, :, 1], vst[:, 1, u], pT[:, u, 2, heads], start=False, stop=True)
                    t.then_inc(pv_pe, 1)

            def attention(i, first, last):
                q = 3 + i
                hT, lT = (oThi, oTlo) if last else (hThi, hTlo)

                def piece(s, halves=(0, 1)):
                    if last:
                        pe.wait_ge(oT_ready, 2 * s + 2)
                    project(q, s, hT, lT, 0, half_done, (half_evac, 2 * (3 + i) - 1), halves=halves)

                piece(0)
                if not first:
                    pe.wait_ge(sc_read, 4 * i)
                    reduce(8 + 2 * i, 0, MCOL2)
                    p_turned(i - 1, 9 + 2 * i)
                piece(1)
                pe.wait_ge(rope_c, 2 + i)
                if not first:
                    pe.wait_ge(pt_act, 6 * i)
                for pr in range(4):
                    for b in range(HB):
                        t = turn(ps[:, 2 + pr // 2, ((pr % 2) * 2 + b) * P:((pr % 2) * 2 + b + 1) * P],
                                 qr[:, b, pr * P:(pr + 1) * P])
                    if pr % 2:
                        t.then_inc(qk_pe, 1)
                pe.wait_ge(k_staged, 2 * i + 2)
                for u in range(2):
                    for b in range(HB):
                        t = turn(ps[:, 4, (2 * u + b) * P:(2 * u + b + 1) * P],
                                 kst[:, b, u].rearrange("p c d -> p (c d)"))
                t.then_inc(qk_pe, 1)
                if not first:
                    outputs(i - 1)
                piece(2, (0,))
                reduce(9 + 2 * i, 1)
                pe.wait_ge(qT_done, 2 * i + 2)
                pe.wait_ge(kT_done, i + 1)
                for u in range(2):
                    if not first:
                        pe.wait_ge(oT_ready, 2 * (i - 1) + u + 1)
                    for e in range(2):
                        rows = slice(e * HD, (e + 1) * HD)
                        if u == 0 and e == 1:
                            pe.wait_ge(mod_added, 10 + 2 * i)
                        for m in range(2):
                            pr = 2 * u + m
                            mm(ps[:, 2 + e, (2 * u + m) * P:(2 * u + m + 1) * P], qT[rows, pr, 0:P],
                               kT[rows, u, 0:P], start=True, stop=True)
                            t = mm(ps[:, 4 + 2 * u + e, m * 192:(m + 1) * 192], qT[rows, pr, P:2 * P],
                                   kT[rows, u, CHUNK:], start=True, stop=True)
                    t.then_inc(sc_pe, 1)
                piece(2, (1,))
                if last:
                    pe.wait_ge(sc_read, 4 * i + 4)
                    p_turned(i, 10 + 2 * i)
                    outputs(i)
                    reduce(10 + 2 * i, 0)
                piece(3)

            attention(0, True, False)
            with pe.Fori(1, 3) as i:
                attention(i, False, False)
            attention(3, False, True)
            reduce(17, 1)

            def spread(src, rnd, bank, n0):
                pe.wait_ge(diag_done, n0 // 2 + rnd + 1)
                for e in range(2):
                    for k in range(4):
                        t = mm(ps[:, bank + e, k * P:(k + 1) * P], ones[:, :], src[:, 4 * e + k],
                               start=True, stop=True)
                    t.then_inc(diag_pe, 1)

            with pe.Fori(1, 3) as w:
                for s in range(4):
                    project(6 + w, s, oThi, oTlo, 0, half_done, (half_evac, 2 * (6 + w) - 1))
                reduce(17 + w, 0)
            for s in range(4):
                project(9, s, oThi, oTlo, 0, half_done, (half_evac, 17))
                if s == 0:
                    spread(diag1, 0, 2, 0)
                if s == 2:
                    pe.wait_ge(grow_done, 2)
                    spread(diag1, 1, 2, 0)
            for b in range(HB):
                pe.wait_ge(n2_done, b + 1)
                for r in range(4):
                    n = 4 * b + r
                    if n >= 4 and H2_BANKS[n] in H2_BANKS[:n]:
                        pe.wait_ge(hf2, H2_BANKS.index(H2_BANKS[n]) + 1)
                    if n == 0:
                        pe.wait_ge(grow_done, 4)
                        pe.wait_ge(mod_added, 20)
                    for t in range(4):
                        last = turn(ps[:, H2_BANKS[n], t * P:(t + 1) * P], y[:, b, (4 * r + t) * P:(4 * r + t + 1) * P])
                    last.then_inc(n2_pe, 1)

            def gu_turn(i):
                for b in range(HB):
                    pe.wait_ge(gu_done, 2 * (i - 1) + b + 1)
                    for t in range(4):
                        last = turn(ps[:, 6 + b, t * P:(t + 1) * P], gu[:, b, t * P:(t + 1) * P])
                    last.then_inc(gu_pe, 1)

            def f1(i, first, with_mod, tail):
                q = 10 + 2 * i
                for s in range(4):
                    if first:
                        pe.wait_ge(h2_ready, 4 + s + 1)
                    free = (half_evac, 19) if first else (silu_done, 2 * i - 1)
                    project(q, s, hThi, hTlo, 0, f_half, free)
                    if s == 1 and not first:
                        gu_turn(i)
                for s in range(4):
                    project(q + 1, s, hThi, hTlo, 2, f_half, None if first else (gu_done, 2 * i - 1))
                    if with_mod and s == 2:
                        reduce(GT_F - 1 + i, 0)
                    if tail and s == 0:
                        spread(diag3, 0, 4, 4)
                    if tail and s == 2:
                        pe.wait_ge(grow_done, 6)
                        spread(diag3, 1, 4, 4)

            f1(0, True, False, False)
            with pe.Fori(1, 5) as i:
                f1(i, False, True, False)
            with pe.Fori(5, FB - 1) as i:
                f1(i, False, False, False)
            f1(FB - 1, False, False, True)
            gu_turn(FB)

            def f2(i, first, end):
                for s in range(4):
                    pe.wait_ge(gk_hi, 4 * i + s + 1)
                    pe.wait_ge(gk_lo, 4 * i + s + 1)
                    split_ready(G_F2 // 4 + i, s)
                    for b in range(HB):
                        tok = slice(b * P, (b + 1) * P)
                        for n in range(NB):
                            if first and s == 0 and b == 0 and n == 0:
                                pe.wait_ge(silu_done, 2 * FB)
                            if first and s == 0 and b == 0 and n == 2:
                                pe.wait_ge(gu_done, 2 * FB)
                            if first and s == 0 and b == 1 and n == 0:
                                pe.wait_ge(grow_done, 8)
                            if first and s == 0 and b == 1 and n == 2:
                                pe.wait_ge(guT_done, 2 * FB)
                            last = three(ps[:, 4 * b + n], hThi[:, s, tok], hTlo[:, s, tok], s, n,
                                         first and s == 0, end and s == 3)
                        if end and s == 3:
                            last.then_inc(y2_half, 1)
                    if not (end and s == 3):
                        last.then_inc(pe_done, 1)

            f2(0, True, False)
            with pe.Fori(1, FT // 4 - 1) as i:
                f2(i, False, False)
            f2(FT // 4 - 1, False, True)


SETUP_ANGLES = 17
F_MOD = [(0, 1), (2,), (3,), (4, 5), (6,), (7,), (), ()]
H2_BANKS = [2, 3, 4, 5, 6, 7, 2, 3]


def kernel(**inputs):
    import numpy as np
    import concourse.bacc as bacc
    from concourse import mybir as mb
    from concourse.bass_utils import run_bass_kernel_spmd as run

    def cols(a):
        return np.ascontiguousarray(a.reshape(-1, P).T)

    x = np.ascontiguousarray(inputs["x"])[0]
    gains = np.stack([cols(inputs["norm_g"][0, n]) for n in range(4)], axis=1)
    power = np.arange(0, HD, 2, dtype=np.float32) / np.float32(HD)
    invf = (np.float32(1.0) / np.power(np.float32(10000.0), power)).astype(np.float32)
    sinks = np.asarray(inputs["swa_sinks"])[0].reshape(4, 2, 2, 2).transpose(0, 1, 3, 2)
    sinks = np.repeat(sinks[:, :, None], HB, axis=2).reshape(1, 2 * QH)
    arrays = {
        "x": x,
        "cT": cols(inputs["c"][0]),
        "pos": np.ascontiguousarray(np.asarray(inputs["positions"])[0].reshape(HB, P).T),
        "invf": np.ascontiguousarray(np.broadcast_to(invf, (P, HALF))),
        "mod_w": np.ascontiguousarray(inputs["mod_w"][0]),
        "modbT": cols(inputs["mod_b"][0]),
        "gT": np.ascontiguousarray(gains),
        "w_qkv": np.ascontiguousarray(inputs["swa_w_qkv"][0]),
        "w_o": np.ascontiguousarray(inputs["swa_w_o"][0]),
        "sinks": np.ascontiguousarray(np.broadcast_to(sinks, (P, 2 * QH))),
        "w_in": np.ascontiguousarray(inputs["ffn_w_in"][0]),
        "w_out": np.ascontiguousarray(inputs["ffn_w_out"][0]),
    }
    nc = bacc.Bacc("TRN2", target_bir_lowering=False, num_devices=1)
    feed, args = {}, []
    for name, a in arrays.items():
        feed[f"in_{name}"] = a
        args.append(nc.dram_tensor(f"in_{name}", a.shape, mb.dt.from_np(a.dtype), kind="ExternalInput").ap())
    args.append(nc.dram_tensor("out_0", (T, D), mb.dt.float32, kind="ExternalOutput").ap())
    build(nc, *args)
    r = run(nc, [feed], core_ids=[0])
    return r.results[0]["out_0"].reshape(1, T, D)
```

```python
from contextlib import ExitStack

import concourse.bass as bass
from concourse import mybir

P = 128
F32 = mybir.dt.float32
F32R = mybir.dt.float32r
I32 = mybir.dt.int32
ACT = mybir.ActivationFunctionType
ALU = mybir.AluOpType
AX = mybir.AxisListType

D = 2048
T = 256
HB = T // P
KT = D // P
N = 512
NB = D // N
HD = 64
HALF = HD // 2
CHUNK = 64
QH = D // HD
KVH = 8
KVW = KVH * HD
F = 5632
FB = F // N
FT = F // P
SCALE = float(HD) ** -0.5
RMS_EPS = 1e-6
MASKED = -1e30
WP = 4
WRING = 4
SRING = 2
MP = 2
MPN = KT // MP
MRING = 4
G_F1 = 40
G_F2 = G_F1 + 2 * WP * FB
SH_M, SC_M, GT_M, SH_F, SC_F, GT_F = (NB * n for n in range(6))
PI_IN = 3.1415925
TWO_PI = (6.28125, 0.0019350051879882812, 3.0199188e-07)
ROUND = 12582912.0


def after(q, s, n=1):
    return q + (s + n) // 4, (s + n) % 4


def build(nc, x, cT, pos, invf, mod_w, modbT, gT, w_qkv, w_o, sinks, w_in, w_out, out):
    with ExitStack() as ctx:
        def sb(name, shape, dt=F32):
            return ctx.enter_context(nc.sbuf_tensor(name, shape, dt))

        def sem(name):
            return ctx.enter_context(nc.semaphore(name))

        raw = sb("raw", [P, WRING, WP, N])
        whi = sb("whi", [P, SRING, WP, N], F32R)
        wlo = sb("wlo", [P, SRING, WP, N], F32R)
        mraw = sb("mraw", [P, MRING, MP, N])
        acc = sb("acc", [P, 2, 2, N])
        hThi = sb("hThi", [P, KT, T], F32R)
        hTlo = sb("hTlo", [P, KT, T], F32R)
        ident = sb("ident", [P, P])
        ones = sb("ones", [P, P])
        ccol = sb("ccol", [P, KT])
        gcol = sb("gcol", [P, 4, KT])
        mbias = sb("mbias", [P, 6 * KT])
        modT = sb("modT", [P, 6 * KT])
        acol = sb("acol", [P, KT])
        vcol = sb("vcol", [P, KT])
        ropeC = sb("ropeC", [P, HB, HD])
        ropeS = sb("ropeS", [P, HB, HD])
        mask = sb("mask", [P, 3 * CHUNK])
        sinkp = sb("sinkp", [P, 2 * QH])
        sinkn = sb("sinkn", [P, 2 * QH])
        ssq = sb("ssq", [P, HB, NB])
        stat = sb("stat", [P, 16])
        rstd = sb("rstd", [P, 8])
        mhalf = sb("mhalf", [P, 1])
        kst = sb("kst", [P, HB, 2, 2, HD])
        vst = sb("vst", [P, HB, 2, HD])
        negm = sb("negm", [P, 2, HB, 4])
        esink = sb("esink", [P, 2, HB, 4])
        mx = sb("mx", [P, 2, HB, 4])
        den = sb("den", [P, 2, HB, 4])

        base = (nc.sbuf_base + 31) // 32 * 32
        ctx.enter_context(nc.sbuf_tensor("arena", [P, 80 * 256], F32))

        def at(name, kb, shape, dt=F32):
            return nc.alloc_sbuf_tensor_at(name, shape, dt, offset=base + int(kb * 1024))

        x0 = at("x0", 32, [P, HB, D])
        nT = at("nT", 48, [P, KT, T])
        posi = at("posi", 72, [P, HB], I32)
        posf = at("posf", 73, [P, HB])
        freq = at("freq", 74, [P, HALF])
        oThi = at("oThi", 0, [P, KT, T], F32R)
        oTlo = at("oTlo", 16, [P, KT, T], F32R)
        qs = at("qs", 32, [P, HB, N])
        qr = at("qr", 36, [P, HB, N])
        kr = at("kr", 40, [P, HB, KVW])
        qT = at("qT", 44, [P, 4, T])
        kT = at("kT", 48, [P, 2, T])
        s0 = at("s0", 50, [P, 2, 4, P])
        s1 = at("s1", 54, [P, 2, 4, 2 * P])
        pT = at("pT", 62, [P, 2, 3, 4, P])
        vr = at("vr", 74, [P, HB, KVW])
        rtmp = at("rtmp", 62, [P, HB, N])
        y = at("y", 32, [P, HB, D])
        x1 = at("x1", 48, [P, HB, D])
        grow = at("grow", 64, [P, D])
        diag1 = at("diag1", 72, [P, 8, P])
        junk = at("junk", 76, [P, N])
        hf = at("hf", 76, [P, 2, 4 * P])
        guT = at("guT", 0, [P, FT, T])
        diag3 = at("diag3", 44, [P, 8, P])
        sg = at("sg", 72, [P, HB, N])
        gu = at("gu", 76, [P, HB, N])

        ps = ctx.enter_context(nc.psum_tensor("ps", [P, 8, N], F32))

        def gated(b, e):
            k = 16 + 2 * (NB * b + e)
            return guT[:, k:k + 2].rearrange("p k t -> p (k t)")

        w_loaded = [sem(f"w_loaded{s}") for s in range(WRING)]
        hi_done, lo_done, lop_done = sem("hi_done"), sem("lo_done"), sem("lop_done")
        pe_done = sem("pe_done")
        m_loaded = [sem(f"m_loaded{s}") for s in range(MRING)]
        acc_step = sem("acc_step")
        joined, reduced, mod_added = sem("joined"), sem("reduced"), sem("mod_added")
        c_in, k_in, x_in, x1_in = sem("c_in"), sem("k_in"), sem("x_in"), sem("x1_in")
        consts = sem("consts")
        id_zero, id_done = sem("id_zero"), sem("id_done")
        silu_c = sem("silu_c")
        setup = sem("setup")
        sines = sem("sines")
        tables = sem("tables")
        xsq, xms, xrs, xn, xt, nT_done = (sem(n) for n in ("xsq", "xms", "xrs", "xn", "xt", "nT_done"))
        a1, hf_done, hhi_done, h_ready = (sem(n) for n in ("a1", "hf_done", "hhi_done", "h_ready"))
        half_done, half_evac = sem("half_done"), sem("half_evac")
        rope_a, rope_b, rope_c = sem("rope_a"), sem("rope_b"), sem("rope_c")
        zeros, k_staged, v_staged = sem("zeros"), sem("k_staged"), sem("v_staged")
        qk_pe, qT_done, kT_done = sem("qk_pe"), sem("qT_done"), sem("kT_done")
        sc_pe, sc_read, rmax, m_ready, es_sum, es_done = (
            sem(n) for n in ("sc_pe", "sc_read", "rmax", "m_ready", "es_sum", "es_done"))
        p_exp, den_sum, r_ready, p_act, p_pool = (
            sem(n) for n in ("p_exp", "den_sum", "r_ready", "p_act", "p_pool"))
        pt_pe, pt_act = sem("pt_pe"), sem("pt_act")
        pv_pe, oThi_done, oT_ready = sem("pv_pe"), sem("oThi_done"), sem("oT_ready")
        vc, diag_done, diag_pe, grow_done = sem("vc"), sem("diag_done"), sem("diag_pe"), sem("grow_done")
        ysq, ychain, yms, yrs, z_done = sem("ysq"), sem("ychain"), sem("yms"), sem("yrs"), sem("z_done")
        x1_done, x1sq, n2_act, n2_dve, n2_pe = (sem(n) for n in ("x1_done", "x1sq", "n2_act", "n2_dve", "n2_pe"))
        hf2, hhi2, h2_ready, h2p_ready, a2 = (sem(n) for n in ("hf2", "hhi2", "h2_ready", "h2p_ready", "a2"))
        f_half, silu_done, gu_done, gu_pe, guT_done = (
            sem(n) for n in ("f_half", "silu_done", "gu_done", "gu_pe", "guT_done"))
        gk_hi, gk_lo = sem("gk_hi"), sem("gk_lo")
        y2_bank, y2sq, y2sum, y2ms, y2rs, y2_step, y2_pool, stored = (
            sem(n) for n in ("y2_bank", "y2sq", "y2sum", "y2ms", "y2rs", "y2_step", "y2_pool", "stored"))

        MCOL0, MCOL, MCOL2 = 6, 5, 7

        block = ctx.enter_context(nc.Block())

        @block.sync
        def _(sp):
            def load_w(q, s, src, first=False):
                if not first:
                    for done in (hi_done, lo_done, lop_done):
                        sp.wait_ge(done, 4 * q + s - 3)
                sp.dma_start(raw[:, s], src).then_inc(w_loaded[s], 16)

            def load_m(n, j, col=None, first=False):
                if not first:
                    sp.wait_ge(acc_step, MP * (MPN * n + j - 3))
                c = n if col is None else col
                src = mod_w.rearrange("(j t p) n -> j p t n", p=P, t=MP)[j][:, :, bass.ds(c * N, N)]
                sp.dma_start(mraw[:, j % 4], src).then_inc(m_loaded[j % 4], 16)

            def block_src(w, r, col):
                return w.rearrange("(r t p) n -> r p t n", p=P, t=WP)[r][:, :, bass.ds(col, N)]

            sp.dma_start(ccol[:, :], cT).then_inc(c_in, 16)
            def load_first_w(g):
                load_w(g // 4, g % 4, block_src(w_qkv, g // 3, (D, D + KVW, 0)[g % 3]), first=g < 4)

            for c in range(4):
                for u in range(2):
                    for j in range(MPN):
                        if (u, j) == (0, 2) and c:
                            load_first_w(3 * c - 1)
                        if (u, j) == (1, 4):
                            load_first_w(3 * c)
                        load_m(2 * c + u, j, (SH_M, SC_M)[u] + c, first=c == u == 0 and j < 4)
                load_first_w(3 * c + 1)
            for j in range(MPN):
                if j == 2:
                    load_first_w(11)
                if j == 4:
                    load_w(3, 0, block_src(w_qkv, 0, N))
                load_m(8, j)
            load_w(3, 1, block_src(w_qkv, 1, N))
            load_w(3, 2, block_src(w_qkv, 2, N))

            def beside(i, w, cols, n, last=False):
                for k in range(16):
                    if k == 4:
                        load_w(i, 3, block_src(w[0], 3, cols[0]))
                    if k == 12:
                        load_w(i + 1, 0, block_src(w[1], 0, cols[1]))
                    load_m(n + k // 8, k % 8)
                load_w(i + 1, 1, block_src(w[1], 1, cols[1]))
                if last:
                    for k in range(8):
                        load_m(n + 2, k)
                load_w(i + 1, 2, block_src(w[1], 2, cols[1]))

            with sp.Fori(0, 2) as i:
                beside(i + 3, (w_qkv, w_qkv), ((i + 1) * N, (i + 2) * N), 9 + 2 * i)
            beside(5, (w_qkv, w_o), (3 * N, 0), 13)
            beside(6, (w_o, w_o), (0, N), 15, last=True)
            with sp.Fori(1, 3) as i:
                for s in range(4):
                    q, r = (6 + i, 3) if s == 0 else (7 + i, s - 1)
                    load_w(q, r, block_src(w_o, r, i * N if s == 0 else (i + 1) * N))
                    for e in range(2):
                        load_m(17 + i, 2 * s + e)
            load_w(9, 3, block_src(w_o, 3, 3 * N))
            load_w(10, 0, block_src(w_in, 0, 0))
            sp.wait_ge(oT_ready, 8)
            for b in range(HB):
                sp.dma_start(x1[:, b], x[b * P:(b + 1) * P, :]).then_inc(x1_in, 16)
            for s in range(1, 4):
                load_w(10, s, block_src(w_in, s, 0))

            def f1_ahead(i, with_mod):
                for u in range(2):
                    for s in range(4):
                        col = F + i * N if u == 0 else (i + 1) * N
                        load_w(11 + 2 * i + u, s, block_src(w_in, s, col))
                        if with_mod:
                            for j in F_MOD[4 * u + s]:
                                load_m(GT_F - 1 + i, j)

            f1_ahead(0, False)
            with sp.Fori(1, 5) as i:
                f1_ahead(i, True)
            with sp.Fori(5, FB - 1) as i:
                f1_ahead(i, False)
            for s in range(4):
                load_w(11 + 2 * (FB - 1), s, block_src(w_in, s, F + (FB - 1) * N))
            with sp.Fori(0, FT // 4) as i:
                for s in range(4):
                    src = w_out.rearrange("(k s p) (a n) -> s p k a n", p=P, s=4, n=N)[s][:, bass.ds(i, 1)]
                    load_w(G_F2 // 4 + i, s, src)
            for b in range(HB):
                for e in range(NB):
                    if e < POOL_ADDS[b]:
                        sp.wait_ge(y2_pool, POOL_ADDS[0] * b + e + 1)
                    else:
                        sp.wait_ge(y2_step, 5 * b + NB + e - POOL_ADDS[b] + 1)
                    cs = slice(e * N, (e + 1) * N)
                    sp.dma_start(out[b * P:(b + 1) * P, cs], x1[:, b, cs]).then_inc(stored, 16)
            sp.wait_ge(stored, 16 * NB * HB)

        @block.scalar
        def _(act):
            A = nc.scalar.activation

            def hi(q, s):
                act.wait_ge(w_loaded[s], 16 * (q + 1))
                if not (isinstance(q, int) and 4 * q + s < SRING):
                    act.wait_ge(pe_done, 4 * q + s - 1)
                A(whi[:, s % 2], raw[:, s], ACT.Copy).then_inc(hi_done, 1)

            for dst, src in ((posi, pos), (freq, invf), (gcol, gT), (mbias, modbT), (sinkp, sinks)):
                act.dma_start(dst[:], src).then_inc(k_in, 16)
            for b in range(HB):
                act.dma_start(x0[:, b], x[b * P:(b + 1) * P, :]).then_inc(x_in, 16)
            act.wait_ge(c_in, 16)
            A(ccol[:, :], ccol[:, :], ACT.Silu).then_inc(silu_c, 1)
            act.wait_ge(x_in, 32)
            for b in range(HB):
                A(nT[:, 8 * b:8 * b + 8].rearrange("p k t -> p (k t)"), x0[:, b], ACT.Square,
                  accum_out=ssq[:, b, 0:1]).then_inc(xsq, 1)
            for b in range(HB):
                act.wait_ge(xrs, b + 1)
                A(x0[:, b], x0[:, b], ACT.Copy, scale=rstd[:, b:b + 1]).then_inc(xn, 1)
            for b in range(HB):
                for r in range(4):
                    act.wait_ge(xt, 4 * b + r + 1)
                    A(nT[:, 4 * r:4 * r + 4, b * P:(b + 1) * P],
                      ps[:, 4 * b + r].rearrange("p (k t) -> p k t", t=P), ACT.Copy).then_inc(nT_done, 1)
            act.wait_ge(setup, 12)
            A(ropeC[:, :, 0:HALF], ropeC[:, :, 0:HALF], ACT.Sin).then_inc(sines, 1)
            A(ropeS[:, :, HALF:], ropeS[:, :, HALF:], ACT.Sin).then_inc(sines, 1)

            def half_ready(sig, count, q, b):
                if b == 0:
                    act.wait_ge(sig, count)
                else:
                    act.wait_ge(pe_done, 4 * q + 4)

            for c in range(4):
                act.wait_ge(hf_done, c + 1)
                A(hThi[:, 4 * c:4 * c + 4], nT[:, 4 * c:4 * c + 4], ACT.Copy).then_inc(hhi_done, 1)
                for g in range(3 * c, 3 * c + 3):
                    hi(g // 4, g % 4)
            for e, dst in enumerate((qs, vr, qs)):
                for b in range(HB):
                    act.wait_ge(half_done if b == 0 else pe_done, e + 1 if b == 0 else 10 + e)
                    if e == 2 and b == 0:
                        act.wait_ge(rope_c, 1)
                    A(dst[:, b], ps[:, 2 * e + b], ACT.Copy).then_inc(half_evac, 1)
                if e == 0:
                    hi(3, 0)

            def probs(i, u, between=None):
                act.wait_ge(m_ready, 2 * i + u + 1)
                for b in range(HB):
                    for h in range(4):
                        s = s0[:, u, h] if b == 0 else s1[:, u, h, CHUNK:]
                        p = A(s, s, ACT.Exp, bias=negm[:, u, b, h:h + 1], scale=SCALE,
                              accum_out=den[:, u, b, h:h + 1])
                    if b == 0 and between is not None:
                        between()
                p.then_inc(p_exp, 1)
                act.wait_ge(es_sum, 2 * i + u + 1)
                A(esink[:, u], esink[:, u], ACT.Exp).then_inc(es_done, 1)

            def normalise(i):
                act.wait_ge(r_ready, 2 * i + 2)
                for b in range(HB):
                    for h in range(4):
                        s = s1[:, 1, h, CHUNK:] if b else s0[:, 1, h]
                        p = A(s, s, ACT.Copy, scale=den[:, 1, b, h:h + 1])
                    p.then_inc(p_act, 1)

            def pT_out(i):
                for u in range(2):
                    for part in range(3):
                        act.wait_ge(pt_pe, 6 * i + 3 * u + part + 1)
                        A(pT[:, u, part].rearrange("p h t -> p (h t)"), ps[:, 3 + 2 * u + part if part else 2 + u],
                          ACT.Copy).then_inc(pt_act, 1)

            def oT_out(i):
                for u in range(2):
                    act.wait_ge(pv_pe, 2 * i + u + 1)
                    A(oThi[:, bass.ds(4 * i + 2 * u, 2)].rearrange("p a t -> p (a t)"), ps[:, 6 + u],
                      ACT.Copy).then_inc(oThi_done, 1)

            def attention(i, first, last):
                q = 3 + i
                hi(*after(q, 0))
                if not first:
                    normalise(i - 1)
                hi(*after(q, 1))
                if not first:
                    act.wait_ge(rope_c, i + 2)
                    pT_out(i - 1)
                hi(*after(q, 2))
                for e in range(2):
                    act.wait_ge(qk_pe, 3 * i + e + 1)
                    A(qT[:, 2 * e:2 * e + 2].rearrange("p a t -> p (a t)"), ps[:, 2 + e],
                      ACT.Copy).then_inc(qT_done, 1)
                act.wait_ge(qk_pe, 3 * i + 3)
                A(kT[:].rearrange("p u t -> p (u t)"), ps[:, 4], ACT.Copy).then_inc(kT_done, 1)
                if not first:
                    oT_out(i - 1)
                if last:
                    probs(i, 0)
                    probs(i, 1)
                    hi(*after(q, 3))
                    return

                def evac_q(b):
                    if b == 0:
                        act.wait_ge(rope_c, i + 2)
                    half_ready(half_done, i + 4, q, b)
                    A(qs[:, b], ps[:, b], ACT.Copy).then_inc(half_evac, 1)

                hi(*after(q, 3))
                probs(i, 0, between=lambda: evac_q(0))
                probs(i, 1, between=lambda: evac_q(1))

            def evac_y(w):
                for b in range(HB):
                    half_ready(half_done, 7 + w, 6 + w, b)
                    yb = y[:, b, bass.ds(w * N, N)]
                    A(yb, ps[:, b], ACT.Copy).then_inc(half_evac, 1)
                    act.wait_ge(half_evac, 12 + 2 * w + b + 1)
                    if not (isinstance(w, int) and w == b == 0):
                        act.wait_ge(ysq, 2 * w + b)
                    A(junk[:, :], yb, ACT.Square, accum_out=ssq[:, b, bass.ds(w, 1)]).then_inc(ysq, 1)

            attention(0, True, False)
            with act.Fori(1, 3) as i:
                attention(i, False, False)
            attention(3, False, True)
            normalise(3)
            pT_out(3)
            oT_out(3)
            evac_y(0)

            def grow_evac(rnd, b0, n0):
                for e in range(2):
                    act.wait_ge(diag_pe, n0 + 2 * rnd + e + 1)
                    A(grow[:, bass.ds((2 * rnd + e) * N, N)], ps[:, b0 + e],
                      ACT.Copy).then_inc(grow_done, 1)

            with act.Fori(1, 3) as w:
                for s in range(4):
                    hi(*after(6 + w, s))
                    if s == 1:
                        grow_evac(w - 1, 2, 0)
                evac_y(w)
            for s in range(1, 4):
                hi(9, s)

            def squares_y3(b):
                half_ready(half_done, 10, 9, b)
                A(y[:, b, 3 * N:], ps[:, b], ACT.Square, accum_out=ssq[:, b, 3:4]).then_inc(ysq, 1)

            def squares_x1(b):
                for e in range(4):
                    cs = slice(e * N, (e + 1) * N)
                    act.wait_ge(x1_done, 4 * b + e + 1)
                    A(y[:, b, cs], x1[:, b, cs], ACT.Square, accum_out=ssq[:, b, e:e + 1]).then_inc(x1sq, 1)

            def h2_hi(*steps):
                for n in steps:
                    b, r = H2_STEPS[n]
                    act.wait_ge(hf2, n + 1)
                    A(hThi[:, 4 * r:4 * r + 4, b * P:(b + 1) * P],
                      hf[:, n % 2].rearrange("p (k t) -> p k t", t=P), ACT.Copy).then_inc(hhi2, 1)

            squares_y3(0)
            squares_x1(0)
            hi(10, 0)
            squares_y3(1)
            hi(10, 1)
            h2_hi(0, 1)
            squares_x1(1)
            act.wait_ge(yrs, 4)
            A(y[:, 1, 0:D // 2], x1[:, 1, 0:D // 2], ACT.Copy, scale=rstd[:, 3:4]).then_inc(n2_act, 1)
            h2_hi(2, 3, 4, 5)
            hi(10, 2)
            h2_hi(6, 7)

            def f1(i, first, tail):
                q = 10 + 2 * i
                for u in range(2):
                    for s in range(4):
                        if tail and u == 1 and s == 3:
                            gk(0, 0)
                        if not (first and u == 0 and s < 2):
                            hi(*after(q + u, s))
                        if u == 0 and s == 1 and not first:
                            act.wait_ge(gu_pe, 2 * i - 1)
                            A(guT[:, bass.ds(4 * i - 4, 4), 0:P],
                              ps[:, 6].rearrange("p (k t) -> p k t", t=P), ACT.Copy).then_inc(guT_done, 1)
                        if u == 0 and s == 3:
                            if not first:
                                act.wait_ge(gu_done, 2 * i)
                            for b in range(HB):
                                half_ready(f_half, 2 * i + 1, q, b)
                                A(sg[:, b], ps[:, b], ACT.Silu).then_inc(silu_done, 1)
                        if tail and u == 1 and s in (0, 2):
                            grow_evac(s // 2, 4, 4)

            def gk(i, s):
                act.wait_ge(pe_done, G_F2 + 4 * i + s - 3)
                if isinstance(i, int) and i == 0 and s == 0:
                    act.wait_ge(guT_done, 2 * (FB - 1))
                A(hThi[:, s], guT[:, bass.ds(4 * i + s, 1)].rearrange("p k t -> p (k t)"),
                  ACT.Copy).then_inc(gk_hi, 1)

            f1(0, True, False)
            with act.Fori(1, FB - 1) as i:
                f1(i, False, False)
            f1(FB - 1, False, True)
            act.wait_ge(gu_pe, 2 * FB - 1)
            A(guT[:, 4 * FB - 4:4 * FB, 0:P], ps[:, 6].rearrange("p (k t) -> p k t", t=P),
              ACT.Copy).then_inc(guT_done, 1)
            q2 = G_F2 // 4

            def f2(i, end=False):
                for s in range(4):
                    if s < 3:
                        gk(i, s + 1)
                        hi(*after(q2 + i, s))
                    elif not end:
                        gk(i + 1, 0)
                        hi(*after(q2 + i, s))

            f2(0)
            with act.Fori(1, FT // 4 - 1) as i:
                f2(i)
            act.wait_ge(guT_done, 2 * FB)
            f2(FT // 4 - 1, end=True)
            for n in range(HB * NB):
                act.wait_ge(y2_bank, n + 1)
                A(guT[:, 2 * n:2 * n + 2].rearrange("p k t -> p (k t)"), ps[:, n], ACT.Square,
                  accum_out=ssq[:, n // NB, n % NB:n % NB + 1]).then_inc(y2sq, 1)

        @block.vector
        def _(dve):
            V = nc.vector

            def lo(q, s, n=2):
                dve.wait_ge(hi_done, 4 * q + s + 1)
                V.tensor_tensor(wlo[:, s % 2, 0:n], raw[:, s, 0:n], whi[:, s % 2, 0:n].bitcast(F32),
                                ALU.subtract).then_inc(lo_done, 1)

            def mod(n, j, a, waits):
                dve.wait_ge(m_loaded[j % 4], 16 * (2 * n + j // 4 + 1))
                if j == 0 and waits is not None:
                    dve.wait_ge(reduced, waits)
                for t in range(MP):
                    k = MP * j + t
                    c = ccol[:, k:k + 1]
                    if k < 2:
                        ins = V.tensor_scalar(acc[:, a, t], mraw[:, j % 4, t], c, None, ALU.mult)
                    else:
                        dve.wait_ge(acc_step, KT * n + k - 1)
                        ins = V.scalar_tensor_tensor(acc[:, a, t], mraw[:, j % 4, t], c, acc[:, a, t],
                                                     ALU.mult, ALU.add)
                    ins.then_inc(acc_step, 1)

            def mod_add(n, bank=MCOL):
                dve.wait_ge(reduced, n + 1)
                V.tensor_tensor(modT[:, bass.ds(4 * n, 4)], ps[:, bank, 0:4], mbias[:, bass.ds(4 * n, 4)],
                                ALU.add).then_inc(mod_added, 1)

            count = [0]

            def link(ins):
                count[0] += 1
                ins.then_inc(setup, 1)
                dve.wait_ge(setup, count[0])

            V.memset(ones[:, :], 1.0)
            V.memset(mhalf[:, :], -0.5)
            V.memset(mask[0:CHUNK, 0:2 * CHUNK], 0.0)
            V.memset(mask[CHUNK:P, CHUNK:], 0.0)
            V.memset(mask[CHUNK:P, 0:CHUNK], MASKED)
            V.memset(mask[0:CHUNK, 2 * CHUNK:], MASKED).then_inc(consts, 1)
            def first_mod(n, js):
                for j in js:
                    mod(n, j, n % 2, n - 1 if n >= 2 else None)

            dve.wait_ge(silu_c, 1)
            first_mod(0, range(0, 4))
            dve.wait_ge(k_in, 80)
            link(V.tensor_copy(posf[:, :], posi[:, :]))
            link(V.tensor_tensor(ropeS[:, :, HALF:], posf[:, :].unsqueeze(2).broadcast_to([P, HB, HALF]),
                                 freq[:, :].unsqueeze(1).broadcast_to([P, HB, HALF]), ALU.mult))
            link(V.tensor_scalar(sinkn[:, :], sinkp[:, :], -1.0, None, ALU.mult))
            turns = ropeC[:, :, HALF:]
            ang, angc = ropeS[:, :, HALF:], ropeC[:, :, 0:HALF]
            link(V.tensor_scalar(angc, ang, 0.0, None, ALU.add))
            for r, shift in ((ang, 0.0), (angc, 0.25)):
                link(V.tensor_scalar(turns, r, 1.0 / (2.0 * 3.141592653589793), shift, ALU.mult, ALU.add))
                link(V.tensor_scalar(turns, turns, ROUND, -ROUND, ALU.add, ALU.add))
                for part in TWO_PI:
                    link(V.scalar_tensor_tensor(r, turns, -part, r, ALU.mult, ALU.add))
            link(V.tensor_scalar(angc, angc, 1.5707963267948966, PI_IN, ALU.add, ALU.min))
            link(V.tensor_scalar(angc, angc, -PI_IN, None, ALU.max))
            link(V.tensor_scalar(ang, ang, PI_IN, -PI_IN, ALU.min, ALU.max))
            assert count[0] == SETUP_ANGLES
            first_mod(0, range(4, 8))
            dve.wait_ge(xsq, 2)
            V.tensor_scalar(stat[:, 12:14], ssq[:, :, 0], 1.0 / D, RMS_EPS, ALU.mult, ALU.add).then_inc(xms, 1)

            def modulate(c):
                ks = slice(4 * c, 4 * c + 4)
                dve.wait_ge(reduced, 2 * c + 2)
                V.tensor_tensor(modT[:, 0:2 * KT].rearrange("p (s k) -> p s k", s=2)[:, :, ks],
                                ps[:, MCOL0, 0:8].rearrange("p (s k) -> p s k", s=2),
                                mbias[:, 0:2 * KT].rearrange("p (s k) -> p s k", s=2)[:, :, ks],
                                ALU.add).then_inc(mod_added, 2)
                dve.wait_ge(mod_added, 2 * c + 2)
                V.scalar_tensor_tensor(acol[:, ks], modT[:, KT + 4 * c:KT + 4 * c + 4], 1.0, gcol[:, 0, ks],
                                       ALU.add, ALU.mult).then_inc(a1, 1)
                dve.wait_ge(a1, c + 1)
                for k in range(4 * c, 4 * c + 4):
                    ins = V.tensor_scalar(nT[:, k], nT[:, k], acol[:, k:k + 1], modT[:, k:k + 1],
                                          ALU.mult, ALU.add)
                ins.then_inc(hf_done, 1)

            def h_lo(c):
                dve.wait_ge(hhi_done, c + 1)
                V.tensor_tensor(hTlo[:, 4 * c:4 * c + 4], nT[:, 4 * c:4 * c + 4],
                                hThi[:, 4 * c:4 * c + 4].bitcast(F32), ALU.subtract).then_inc(h_ready, 1)

            def rope_parts(n, half_count, dst):
                dve.wait_ge(half_evac, half_count)
                V.tensor_tensor(dst.rearrange("p b (h d) -> p b h d", d=HD),
                                qs[:].rearrange("p b (h d) -> p b h d", d=HD),
                                ropeC[:].unsqueeze(2).broadcast_to([P, HB, 8, HD]), ALU.mult).then_inc(rope_a, 1)
                yield
                dve.wait_ge(rope_a, n + 1)
                dve.wait_ge(rope_b, 2 * n + 2)
                V.tensor_tensor(dst, dst, rtmp[:], ALU.add).then_inc(rope_c, 1)
                yield

            for c in range(4):
                if c:
                    first_mod(2 * c, range(0, 4))
                    if c == 1:
                        dve.wait_ge(nT_done, 8)
                    modulate(c - 1)
                    first_mod(2 * c, range(4, 8))
                if c:
                    h_lo(c - 1)
                    for g in (3 * c - 3, 3 * c - 2):
                        lo(g // 4, g % 4)
                first_mod(2 * c + 1, range(0, 4))
                if c:
                    lo((3 * c - 1) // 4, (3 * c - 1) % 4)
                first_mod(2 * c + 1, range(4, 8))
                if c == 0:
                    dve.wait_ge(sines, 2)
                    V.tensor_copy(ropeC[:, :, HALF:], ropeC[:, :, 0:HALF])
                    V.tensor_scalar(ropeS[:, :, 0:HALF], ropeS[:, :, HALF:], -1.0, None,
                                    ALU.mult).then_inc(tables, 1)
            first_mod(8, range(0, 2))
            modulate(3)
            first_mod(8, range(2, 3))
            h_lo(3)
            lo(2, 1)
            lo(2, 2)
            dve.wait_ge(h_ready, 4)
            V.memset(s1[:, :, :, 0:CHUNK], 0.0).then_inc(zeros, 1)
            first_mod(8, range(3, 5))
            lo(2, 3)
            keys = rope_parts(0, 2, kr[:])
            next(keys)
            first_mod(8, range(5, 8))
            next(keys)
            lo(3, 0)

            def max_and_sinks(i, between=None):
                def second(u):
                    V.tensor_tensor(s1[:, u, :, CHUNK:].rearrange("p (e m) k -> p e m k", e=2),
                                    ps[:, 4 + 2 * u:6 + 2 * u, 0:6 * CHUNK].rearrange("p e (m k) -> p e m k", m=2),
                                    mask[:].unsqueeze(1).unsqueeze(1).broadcast_to([P, 2, 2, 3 * CHUNK]),
                                    ALU.add).then_inc(sc_read, 1)

                def first_half(u):
                    V.tensor_tensor(s0[:, u].rearrange("p (e m) k -> p e m k", e=2),
                                    ps[:, 2:4, u * 256:(u + 1) * 256].rearrange("p e (m k) -> p e m k", m=2),
                                    mask[:, CHUNK:].unsqueeze(1).unsqueeze(1).broadcast_to([P, 2, 2, P]),
                                    ALU.add).then_inc(sc_read, 1)

                for u in range(2):
                    dve.wait_ge(sc_pe, 2 * i + u + 1)
                    second(u)
                    if u == 0:
                        dve.wait_ge(sc_pe, 2 * i + 2)
                    first_half(u)
                    if u == 1 and between is not None:
                        between()
                    dve.wait_ge(sc_read, 4 * i + 2 * u + 2)
                    V.tensor_reduce(mx[:, u, 0], s0[:, u], AX.X, ALU.max).then_inc(rmax, 1)
                    V.tensor_reduce(mx[:, u, 1], s1[:, u, :, CHUNK:], AX.X, ALU.max).then_inc(rmax, 1)
                    dve.wait_ge(rmax, 4 * i + 2 * u + 2)
                    V.scalar_tensor_tensor(negm[:, u].rearrange("p b h -> p (b h)"),
                                           mx[:, u].rearrange("p b h -> p (b h)"), -SCALE,
                                           sinkn[:, bass.ds(16 * i + 8 * u, 8)], ALU.mult,
                                           ALU.min).then_inc(m_ready, 1)
                    dve.wait_ge(m_ready, 2 * i + u + 1)
                    V.tensor_tensor(esink[:, u].rearrange("p b h -> p (b h)"),
                                    negm[:, u].rearrange("p b h -> p (b h)"),
                                    sinkp[:, bass.ds(16 * i + 8 * u, 8)], ALU.add).then_inc(es_sum, 1)

            def denominator(i, u):
                dve.wait_ge(p_exp, 2 * i + u + 1)
                dve.wait_ge(es_done, 2 * i + u + 1)
                V.tensor_tensor(den[:, u], den[:, u], esink[:, u], ALU.add).then_inc(den_sum, 1)
                dve.wait_ge(den_sum, 2 * i + u + 1)
                V.reciprocal(den[:, u], den[:, u]).then_inc(r_ready, 1)

            def oT_lo(i):
                for u in range(2):
                    dve.wait_ge(oThi_done, 2 * i + u + 1)
                    V.tensor_tensor(oTlo[:, bass.ds(4 * i + 2 * u, 2)].rearrange("p a t -> p (a t)"), ps[:, 6 + u],
                                    oThi[:, bass.ds(4 * i + 2 * u, 2)].rearrange("p a t -> p (a t)").bitcast(F32),
                                    ALU.subtract).then_inc(oT_ready, 1)

            def attention(i, first, last):
                q = 3 + i
                m1, m2 = 9 + 2 * i, 10 + 2 * i

                def m(which, *js):
                    for j in js:
                        n = m1 - 1 + which
                        mod(n, j, which % 2, n - 1)

                turned = rope_parts(1 + i, 2 * (3 + i), qr[:])
                next(turned)
                if not first:
                    denominator(i - 1, 1)
                lo(*after(q, 0), n=ATT_LO[0])
                mod_add(8 + 2 * i, MCOL0 if first else MCOL2)
                next(turned)
                m(1, 0, 1, 2, 3, 4)
                lo(*after(q, 1), n=ATT_LO[1])
                m(1, 5, 6, 7)
                lo(*after(q, 2), n=ATT_LO[2])
                m(2, 0)
                if not first:
                    oT_lo(i - 1)
                if not last:
                    mod_add(m1)
                m(2, 1, 2, 3)
                max_and_sinks(i, None if last else lambda: lo(*after(q, 3), n=ATT_LO[3]))
                if last:
                    mod_add(m1, MCOL2)
                m(2, 4)
                denominator(i, 0)
                m(2, 5)
                if last:
                    denominator(i, 1)
                    lo(*after(q, 3), n=ATT_LO[3])
                m(2, 6, 7)

            attention(0, True, False)
            with dve.Fori(1, 3) as i:
                attention(i, False, False)
            attention(3, False, True)
            V.tensor_tensor(vcol[:, :], modT[:, 2 * KT:3 * KT], gcol[:, 1], ALU.mult).then_inc(vc, 1)
            for j in range(4):
                mod(17, j, 1, 16)
            oT_lo(3)
            mod_add(16)
            for j in range(4, 8):
                mod(17, j, 1, 16)
            with dve.Fori(1, 3) as w:
                for s, js in enumerate(((0, 1, 2), (3, 4), (5, 6), (7,))):
                    lo(*after(6 + w, s))
                    if s == 0:
                        mod_add(16 + w)
                    for j in js:
                        mod(17 + w, j, 1, 17 + w)
            def gate(cols, count):
                dve.wait_ge(grow_done, count)
                V.tensor_tensor(y[:, :, cols], y[:, :, cols],
                                grow[:, cols].unsqueeze(1).broadcast_to([P, HB, cols.stop - cols.start]),
                                ALU.mult).then_inc(z_done, 1)

            def z_last(b):
                dve.wait_ge(ysq, 7 + b)
                V.tensor_tensor(y[:, b, 3 * N:], ps[:, b], grow[:, 3 * N:], ALU.mult).then_inc(z_done, 1)

            def norm_y(b):
                dve.wait_ge(ysq, 7 + b)
                V.tensor_scalar(stat[:, 6 + b:7 + b], ssq[:, b, 3:4], 1.0 / D, stat[:, 4 + b:5 + b], ALU.mult,
                                ALU.add).then_inc(yms, 1)

            def residual(b):
                dve.wait_ge(z_done, 3 + b)
                dve.wait_ge(yrs, 2 * b + 1)
                for e in range(4):
                    cs = slice(e * N, (e + 1) * N)
                    V.scalar_tensor_tensor(x1[:, b, cs], y[:, b, cs], rstd[:, b:b + 1], x1[:, b, cs], ALU.mult,
                                           ALU.add).then_inc(x1_done, 1)
                if b == 1:
                    lo(10, 1)
                dve.wait_ge(x1sq, 4 * b + 4)
                V.tensor_reduce(stat[:, b:b + 1], ssq[:, b], AX.X, ALU.add).then_inc(ychain, 1)
                dve.wait_ge(ychain, 3 + b)
                V.tensor_scalar(stat[:, 8 + b:9 + b], stat[:, b:b + 1], 1.0 / D, RMS_EPS, ALU.mult,
                                ALU.add).then_inc(yms, 1)

            def norm_x1(b, e):
                dve.wait_ge(yrs, 2 * b + 2)
                cs = slice(e * D // 2, (e + 1) * D // 2)
                V.tensor_scalar(y[:, b, cs], x1[:, b, cs], rstd[:, 2 + b:3 + b], None, ALU.mult).then_inc(n2_dve, 1)

            def h2_mod(*steps):
                for n in steps:
                    b, r = H2_STEPS[n]
                    dve.wait_ge(n2_pe, 4 * b + r + 1)
                    if n >= 2:
                        dve.wait_ge(h2p_ready if n % 2 else h2_ready, n // 2)
                    for t in range(4):
                        k = 4 * r + t
                        ins = V.tensor_scalar(hf[:, n % 2, t * P:(t + 1) * P],
                                              ps[:, H2_BANKS[4 * b + r], t * P:(t + 1) * P],
                                              acol[:, k:k + 1], modT[:, 3 * KT + k:3 * KT + k + 1],
                                              ALU.mult, ALU.add)
                    ins.then_inc(hf2, 1)

            def h2_lo(n):
                b, r = H2_STEPS[n]
                dve.wait_ge(hhi2, n + 1)
                V.tensor_tensor(hTlo[:, 4 * r:4 * r + 4, b * P:(b + 1) * P],
                                hf[:, n % 2].rearrange("p (k t) -> p k t", t=P),
                                hThi[:, 4 * r:4 * r + 4, b * P:(b + 1) * P].bitcast(F32),
                                ALU.subtract).then_inc(h2_ready, 1)

            lo(9, 1)
            dve.wait_ge(half_evac, 16)
            dve.wait_ge(ysq, 4)
            gate(slice(0, 2 * N), 4)
            lo(9, 2)
            dve.wait_ge(ysq, 6)
            gate(slice(2 * N, 3 * N), 4)
            V.tensor_reduce(stat[:, 12:14], ssq[:, :, 0:3], AX.X, ALU.add).then_inc(ychain, 1)
            dve.wait_ge(ychain, 1)
            V.tensor_scalar(stat[:, 4:6], stat[:, 12:14], 1.0 / D, RMS_EPS, ALU.mult, ALU.add).then_inc(ychain, 1)
            dve.wait_ge(ychain, 2)
            lo(9, 3)
            mod_add(19)
            dve.wait_ge(mod_added, 20)
            V.scalar_tensor_tensor(acol[:, :], modT[:, 4 * KT:5 * KT], 1.0, gcol[:, 2], ALU.add,
                                   ALU.mult).then_inc(a2, 1)
            dve.wait_ge(x1_in, 32)
            dve.wait_ge(a2, 1)
            norm_y(0)
            z_last(0)
            residual(0)
            norm_x1(0, 0)
            norm_x1(0, 1)
            h2_mod(0)
            lo(10, 0)
            norm_y(1)
            h2_lo(0)
            h2_mod(1)
            z_last(1)
            residual(1)
            norm_x1(1, 1)
            h2_mod(2, 3)
            h2_lo(2)
            h2_mod(4, 5)
            h2_lo(4)
            h2_mod(6)
            lo(10, 2)
            h2_mod(7)
            h2_lo(6)

            def f1(i, first, with_mod, tail):
                q = 10 + 2 * i
                for u in range(2):
                    for s in range(4):
                        if tail and u == 1 and s == 3:
                            gk_low(0, 0)
                        if not (first and u == 0 and s < 2):
                            lo(*after(q + u, s))
                        if u == 0 and s == 1 and not first:
                            dve.wait_ge(gu_pe, 2 * i)
                            V.tensor_copy(guT[:, bass.ds(4 * i - 4, 4), P:2 * P],
                                          ps[:, 7].rearrange("p (k t) -> p k t", t=P)).then_inc(guT_done, 1)
                        if with_mod:
                            for j in F_MOD[4 * u + s]:
                                mod(GT_F - 1 + i, j, 0, GT_F - 1 + i)
                if with_mod:
                    mod_add(GT_F - 1 + i)
                for b in range(HB):
                    if b == 0:
                        dve.wait_ge(f_half, 2 * i + 2)
                    else:
                        dve.wait_ge(pe_done, 4 * (q + 1) + 4)
                    dve.wait_ge(silu_done, 2 * i + b + 1)
                    V.tensor_tensor(gu[:, b], sg[:, b], ps[:, 2 + b], ALU.mult).then_inc(gu_done, 1)

            def gk_low(i, s):
                dve.wait_ge(gk_hi, 4 * i + s + 1)
                V.tensor_tensor(hTlo[:, s], guT[:, bass.ds(4 * i + s, 1)].rearrange("p k t -> p (k t)"),
                                hThi[:, s].bitcast(F32), ALU.subtract).then_inc(gk_lo, 1)

            f1(0, True, False, False)
            with dve.Fori(1, 5) as i:
                f1(i, False, True, False)
            dve.wait_ge(mod_added, 24)
            dve.wait_ge(diag_done, 2)
            V.tensor_tensor(vcol[:, :], modT[:, 5 * KT:6 * KT], gcol[:, 3], ALU.mult).then_inc(vc, 1)
            with dve.Fori(5, FB - 1) as i:
                f1(i, False, False, False)
            f1(FB - 1, False, False, True)
            dve.wait_ge(gu_pe, 2 * FB)
            V.tensor_copy(guT[:, 4 * FB - 4:4 * FB, P:2 * P],
                          ps[:, 7].rearrange("p (k t) -> p k t", t=P)).then_inc(guT_done, 1)
            q2 = G_F2 // 4

            def f2(i, end=False):
                for s in range(4):
                    if s < 3:
                        gk_low(i, s + 1)
                        lo(*after(q2 + i, s))
                    elif not end:
                        gk_low(i + 1, 0)
                        lo(*after(q2 + i, s))

            f2(0)
            with dve.Fori(1, FT // 4 - 1) as i:
                f2(i)
            f2(FT // 4 - 1, end=True)
            for b in range(HB):
                dve.wait_ge(y2sq, NB * (b + 1))
                V.tensor_reduce(stat[:, 2 + b:3 + b], ssq[:, b], AX.X, ALU.add).then_inc(y2sum, 1)
                dve.wait_ge(y2sum, b + 1)
                V.tensor_scalar(stat[:, 10 + b:11 + b], stat[:, 2 + b:3 + b], 1.0 / D, RMS_EPS, ALU.mult,
                                ALU.add).then_inc(y2ms, 1)
                dve.wait_ge(y2rs, b + 1)
                for e in range(NB):
                    V.scalar_tensor_tensor(gated(b, e), ps[:, NB * b + e], rstd[:, 4 + b:5 + b],
                                           grow[:, e * N:(e + 1) * N], ALU.mult, ALU.mult).then_inc(y2_step, 1)
                for e in range(POOL_ADDS[b], NB):
                    cs = slice(e * N, (e + 1) * N)
                    dve.wait_ge(y2_step, 5 * b + e + 1)
                    V.tensor_tensor(x1[:, b, cs], x1[:, b, cs], gated(b, e), ALU.add).then_inc(y2_step, 1)

        @block.gpsimd
        def _(pool):
            G = nc.gpsimd

            def lo(q, s, n=2):
                pool.wait_ge(hi_done, 4 * q + s + 1)
                G.tensor_tensor(wlo[:, s % 2, n:4], raw[:, s, n:4], whi[:, s % 2, n:4].bitcast(F32),
                                ALU.subtract).then_inc(lop_done, 1)

            def inv_root(dst, src, done):
                G.tensor_tensor(dst, src, mhalf[:, :], ALU.pow).then_inc(done, 1)

            G.memset(ident[:, :], 0.0).then_inc(id_zero, 1)
            pool.wait_ge(id_zero, 1)
            G.affine_select(out=ident[:, :], in_=ident[:, :], compare_op=ALU.not_equal, fill=1.0, base=0,
                            pattern=[[-1, P]], channel_multiplier=1).then_inc(id_done, 1)
            pool.wait_ge(consts, 1)
            pool.wait_ge(xms, 1)
            for b in range(HB):
                inv_root(rstd[:, b:b + 1], stat[:, 12 + b:13 + b], xrs)

            def join(n, a):
                pool.wait_ge(acc_step, KT * (n + 1))
                G.tensor_tensor(acc[:, a, 0], acc[:, a, 0], acc[:, a, 1], ALU.add).then_inc(joined, 1)

            def rope(n, half_count):
                pool.wait_ge(half_evac, half_count)
                x4 = qs[:].rearrange("p b (h d) -> p b h d", d=HD)
                t4 = rtmp[:].rearrange("p b (h d) -> p b h d", d=HD)
                for a, b in ((0, HALF), (HALF, 0)):
                    G.tensor_tensor(t4[:, :, :, a:a + HALF], x4[:, :, :, b:b + HALF],
                                    ropeS[:, :, a:a + HALF].unsqueeze(2).broadcast_to([P, HB, 8, HALF]),
                                    ALU.mult).then_inc(rope_b, 1)

            for c in range(4):
                for g in range(3 * c - 3, 3 * c - 1):
                    if c:
                        lo(g // 4, g % 4)
                join(2 * c, 0)
                if c:
                    lo((3 * c - 1) // 4, (3 * c - 1) % 4)
                join(2 * c + 1, 1)
            pool.wait_ge(tables, 1)
            for g in (9, 10, 11):
                lo(g // 4, g % 4)
            rope(0, 2)
            join(8, 0)
            lo(3, 0)

            def normalise(i):
                pool.wait_ge(r_ready, 2 * i + 1)
                for b, p in enumerate((s0[:, 0], s1[:, 0, :, CHUNK:])):
                    G.tensor_tensor(p, p, den[:, 0, b].unsqueeze(2).broadcast_to([P, 4, P + b * CHUNK]),
                                    ALU.mult).then_inc(p_pool, 1)

            def attention(i, first, last):
                q = 3 + i
                rope(1 + i, 2 * (3 + i))
                lo(*after(q, 0), n=ATT_LO[0])
                lo(*after(q, 1), n=ATT_LO[1])
                if first:
                    pool.wait_ge(rope_c, 1)
                else:
                    pool.wait_ge(qk_pe, 3 * i)
                for twin in range(2):
                    G.tensor_copy(kst[:, :, :, twin], kr[:, :, bass.ds(2 * i * HD, 2 * HD)]
                                  .rearrange("p b (h d) -> p b h d", d=HD)).then_inc(k_staged, 1)
                join(9 + 2 * i, 1)
                lo(*after(q, 2), n=ATT_LO[2])
                if first:
                    pool.wait_ge(half_evac, 4)
                else:
                    pool.wait_ge(pv_pe, 2 * i)
                G.tensor_copy(vst[:], vr[:, :, bass.ds(2 * i * HD, 2 * HD)]
                              .rearrange("p b (h d) -> p b h d", d=HD)).then_inc(v_staged, 1)
                if last:
                    normalise(i)
                lo(*after(q, 3), n=ATT_LO[3])
                if not last:
                    normalise(i)
                join(10 + 2 * i, 0)

            attention(0, True, False)
            with pool.Fori(1, 3) as i:
                attention(i, False, False)
            attention(3, False, True)
            join(17, 1)

            def diagonals(dst, rnd):
                G.tensor_tensor(dst[:], ident[:].unsqueeze(1).broadcast_to([P, 8, P]),
                                vcol[:, bass.ds(8 * rnd, 8)].unsqueeze(2).broadcast_to([P, 8, P]),
                                ALU.mult).then_inc(diag_done, 1)

            pool.wait_ge(vc, 1)
            with pool.Fori(1, 3) as w:
                lo(*after(6 + w, 0))
                diagonals(diag1, w - 1)
                for s in range(1, 4):
                    lo(*after(6 + w, s))
                join(17 + w, 1)
            for s in range(1, 4):
                lo(9, s)

            def rstds(n):
                pool.wait_ge(yms, n + 1)
                dst, src = n % 2 * 2 + n // 2, 6 + n % 2 * 2 + n // 2
                inv_root(rstd[:, dst:dst + 1], stat[:, src:src + 1], yrs)

            def h2_lo(n):
                b, r = H2_STEPS[n]
                pool.wait_ge(hhi2, n + 1)
                G.tensor_tensor(hTlo[:, 4 * r:4 * r + 4, b * P:(b + 1) * P],
                                hf[:, n % 2].rearrange("p (k t) -> p k t", t=P),
                                hThi[:, 4 * r:4 * r + 4, b * P:(b + 1) * P].bitcast(F32),
                                ALU.subtract).then_inc(h2p_ready, 1)

            rstds(0)
            rstds(1)
            lo(10, 0)
            rstds(2)
            lo(10, 1)
            h2_lo(1)
            rstds(3)
            h2_lo(3)
            h2_lo(5)
            lo(10, 2)
            h2_lo(7)

            def f1(i, first, with_mod):
                for u in range(2):
                    for s in range(4):
                        if not (first and u == 0 and s < 2):
                            lo(*after(10 + 2 * i + u, s))
                        if with_mod and (u, s) == (1, 1):
                            join(GT_F - 1 + i, 0)

            f1(0, True, False)
            with pool.Fori(1, 5) as i:
                f1(i, False, True)
            with pool.Fori(5, FB - 1) as i:
                f1(i, False, False)
            for s in range(4):
                lo(*after(10 + 2 * (FB - 1), s))
            pool.wait_ge(vc, 2)
            diagonals(diag3, 0)
            for s in range(2):
                lo(*after(11 + 2 * (FB - 1), s))
            pool.wait_ge(diag_pe, 6)
            diagonals(diag3, 1)
            for s in range(2, 4):
                lo(*after(11 + 2 * (FB - 1), s))
            q2 = G_F2 // 4
            with pool.Fori(0, FT // 4 - 1) as i:
                for s in range(4):
                    lo(*after(q2 + i, s))
            for s in range(3):
                lo(*after(q2 + FT // 4 - 1, s))
            for b in range(HB):
                pool.wait_ge(y2ms, b + 1)
                inv_root(rstd[:, 4 + b:5 + b], stat[:, 10 + b:11 + b], y2rs)
                for e in range(POOL_ADDS[b]):
                    cs = slice(e * N, (e + 1) * N)
                    pool.wait_ge(y2_step, 5 * b + e + 1)
                    G.tensor_tensor(x1[:, b, cs], x1[:, b, cs], gated(b, e), ALU.add).then_inc(y2_pool, 1)

        @block.tensor
        def _(pe):
            mm = nc.tensor.matmul

            def split_ready(q, s):
                for done in (hi_done, lo_done, lop_done):
                    pe.wait_ge(done, 4 * q + s + 1)

            def three(dst, hi, lo, s, n, start, stop):
                mm(dst, hi, whi[:, s % 2, n], start=start, stop=False)
                mm(dst, hi, wlo[:, s % 2, n], start=False, stop=False)
                return mm(dst, lo, whi[:, s % 2, n], start=False, stop=stop)

            def project(q, s, hT, lT, bank, half_sig, bank_free=None, slot=None, halves=(0, 1)):
                r = s if slot is None else slot
                split_ready(q, r)
                for b in halves:
                    if s == 0 and bank_free is not None:
                        pe.wait_ge(bank_free[0], bank_free[1] + b)
                    for t in range(WP):
                        k = WP * s + t
                        last = three(ps[:, bank + b], hT[:, k, b * P:(b + 1) * P], lT[:, k, b * P:(b + 1) * P],
                                     r, t, k == 0, k == KT - 1)
                    if s == 3 and b == 0:
                        last.then_inc(half_sig, 1)
                if 1 in halves:
                    last.then_inc(pe_done, 1)

            def turn(dst, src):
                return nc.tensor.transpose(dst, src, ident[:, :])

            def reduce(n, a, bank=MCOL, col=0):
                pe.wait_ge(joined, n + 1)
                if not (col or isinstance(n, int) and n == 0):
                    pe.wait_ge(mod_added, n)
                for f in range(4):
                    last = mm(ps[:, bank, col + f:col + f + 1], acc[:, a, 0, f * P:(f + 1) * P], ones[:, 0:1],
                              start=True, stop=True)
                last.then_inc(reduced, 1)

            pe.wait_ge(id_done, 1)
            pe.wait_ge(consts, 1)
            for b in range(HB):
                pe.wait_ge(xn, b + 1)
                for r in range(4):
                    for t in range(4):
                        last = turn(ps[:, 4 * b + r, t * P:(t + 1) * P], x0[:, b, (4 * r + t) * P:(4 * r + t + 1) * P])
                    last.then_inc(xt, 1)
            pe.wait_ge(nT_done, 8)
            for c in range(4):
                reduce(2 * c, 0, MCOL0)
                reduce(2 * c + 1, 1, MCOL0, 4)
                pe.wait_ge(h_ready, c + 1)
                for e in range(3):
                    g = 3 * c + e
                    project(g // 4, c, hThi, hTlo, 2 * e, half_done, slot=g % 4)
            reduce(8, 0, MCOL0)

            def p_turned(i, added):
                for u in range(2):
                    if u == 0:
                        pe.wait_ge(p_pool, 2 * i + 1)
                    else:
                        pe.wait_ge(p_act, 2 * i + 1)
                    for h in range(4):
                        t = turn(ps[:, 2 + u, h * P:(h + 1) * P], s0[:, u, h])
                    t.then_inc(pt_pe, 1)
                    if u == 0:
                        pe.wait_ge(p_pool, 2 * i + 2)
                    else:
                        pe.wait_ge(p_act, 2 * i + 2)
                    for part in range(2):
                        if u == part == 1:
                            pe.wait_ge(mod_added, added)
                        for h in range(4):
                            t = turn(ps[:, 4 + 2 * u + part, h * P:(h + 1) * P],
                                     s1[:, u, h, part * P:(part + 1) * P])
                        t.then_inc(pt_pe, 1)

            def outputs(i):
                pe.wait_ge(pt_act, 6 * i + 6)
                pe.wait_ge(v_staged, i + 1)
                for u in range(2):
                    for e in range(2):
                        o = ps[e * HD:(e + 1) * HD, 6 + u].rearrange("p (m b t) -> p m b t", m=2, b=HB)
                        heads = slice(2 * e, 2 * e + 2)
                        mm(o[:, :, 0], vst[:, 0, u], pT[:, u, 0, heads], start=True, stop=True)
                        mm(o[:, :, 1], vst[:, 0, u], pT[:, u, 1, heads], start=True, stop=False)
                        t = mm(o[:, :, 1], vst[:, 1, u], pT[:, u, 2, heads], start=False, stop=True)
                    t.then_inc(pv_pe, 1)

            def attention(i, first, last):
                q = 3 + i
                hT, lT = (oThi, oTlo) if last else (hThi, hTlo)

                def piece(s, halves=(0, 1)):
                    if last:
                        pe.wait_ge(oT_ready, 2 * s + 2)
                    project(q, s, hT, lT, 0, half_done, (half_evac, 2 * (3 + i) - 1), halves=halves)

                piece(0)
                if not first:
                    pe.wait_ge(sc_read, 4 * i)
                    reduce(8 + 2 * i, 0, MCOL2)
                    p_turned(i - 1, 9 + 2 * i)
                piece(1)
                pe.wait_ge(rope_c, 2 + i)
                if not first:
                    pe.wait_ge(pt_act, 6 * i)
                for pr in range(4):
                    for b in range(HB):
                        t = turn(ps[:, 2 + pr // 2, ((pr % 2) * 2 + b) * P:((pr % 2) * 2 + b + 1) * P],
                                 qr[:, b, pr * P:(pr + 1) * P])
                    if pr % 2:
                        t.then_inc(qk_pe, 1)
                pe.wait_ge(k_staged, 2 * i + 2)
                for u in range(2):
                    for b in range(HB):
                        t = turn(ps[:, 4, (2 * u + b) * P:(2 * u + b + 1) * P],
                                 kst[:, b, u].rearrange("p c d -> p (c d)"))
                t.then_inc(qk_pe, 1)
                if not first:
                    outputs(i - 1)
                if not last:
                    piece(2, (0,))
                    reduce(9 + 2 * i, 1)
                pe.wait_ge(qT_done, 2 * i + 2)
                pe.wait_ge(kT_done, i + 1)
                for u in range(2):
                    if not first:
                        pe.wait_ge(oT_ready, 2 * (i - 1) + u + 1)
                    for e in range(2):
                        rows = slice(e * HD, (e + 1) * HD)
                        if u == 0 and e == 1 and not last:
                            pe.wait_ge(mod_added, 10 + 2 * i)
                        for m in range(2):
                            pr = 2 * u + m
                            mm(ps[:, 2 + e, (2 * u + m) * P:(2 * u + m + 1) * P], qT[rows, pr, 0:P],
                               kT[rows, u, 0:P], start=True, stop=True)
                            t = mm(ps[:, 4 + 2 * u + e, m * 192:(m + 1) * 192], qT[rows, pr, P:2 * P],
                                   kT[rows, u, CHUNK:], start=True, stop=True)
                    t.then_inc(sc_pe, 1)
                piece(2, (0, 1) if last else (1,))
                if last:
                    pe.wait_ge(sc_read, 4 * i + 4)
                    reduce(9 + 2 * i, 1, MCOL2)
                    p_turned(i, 10 + 2 * i)
                    outputs(i)
                    reduce(10 + 2 * i, 0)
                piece(3)

            attention(0, True, False)
            with pe.Fori(1, 3) as i:
                attention(i, False, False)
            attention(3, False, True)

            def spread(src, rnd, bank, n0):
                pe.wait_ge(diag_done, n0 // 2 + rnd + 1)
                for e in range(2):
                    for k in range(4):
                        t = mm(ps[:, bank + e, k * P:(k + 1) * P], ones[:, :], src[:, 4 * e + k],
                               start=True, stop=True)
                    t.then_inc(diag_pe, 1)

            with pe.Fori(1, 3) as w:
                for s in range(4):
                    project(6 + w, s, oThi, oTlo, 0, half_done, (half_evac, 2 * (6 + w) - 1))
                    if s == 0:
                        reduce(16 + w, 1)
                    if s == 1:
                        spread(diag1, w - 1, 2, 0)
            def project9(s, halves=(0, 1)):
                project(9, s, oThi, oTlo, 0, half_done, (half_evac, 17), halves=halves)

            project9(0)
            project9(1)
            reduce(19, 1)
            for b in range(HB):
                for s in (2, 3):
                    project9(s, (b,))

            def norm_turn(b):
                for r in range(4):
                    if b == 0:
                        pe.wait_ge(n2_dve, r // 2 + 1)
                    elif r // 2:
                        pe.wait_ge(n2_dve, 3)
                    else:
                        pe.wait_ge(n2_act, 1)
                    bank = H2_BANKS[4 * b + r]
                    if bank == 2:
                        pe.wait_ge(grow_done, 4)
                    if b == 1 and bank in H2_BANKS[0:4]:
                        pe.wait_ge(hf2, H2_STEPS.index((0, H2_BANKS.index(bank))) + 1)
                    if b == 0 and bank == MCOL:
                        pe.wait_ge(mod_added, 20)
                    for t in range(4):
                        k = 4 * r + t
                        last = turn(ps[:, bank, t * P:(t + 1) * P], y[:, b, k * P:(k + 1) * P])
                    last.then_inc(n2_pe, 1)

            norm_turn(0)

            def gu_turn(i):
                for b in range(HB):
                    pe.wait_ge(gu_done, 2 * (i - 1) + b + 1)
                    for t in range(4):
                        last = turn(ps[:, 6 + b, t * P:(t + 1) * P], gu[:, b, t * P:(t + 1) * P])
                    last.then_inc(gu_pe, 1)

            def f1(i, first, with_mod, tail):
                q = 10 + 2 * i
                if first:
                    for pair in ((0, 1), (2,), (3,)):
                        for b in range(HB):
                            if b == 1 and pair == (0, 1):
                                norm_turn(1)
                            for s in pair:
                                n = H2_STEPS.index((b, s))
                                pe.wait_ge(h2p_ready if n % 2 else h2_ready, n // 2 + 1)
                                project(q, s, hThi, hTlo, 0, f_half, halves=(b,))
                else:
                    for s in range(4):
                        project(q, s, hThi, hTlo, 0, f_half, (silu_done, 2 * i - 1))
                        if s == 1:
                            gu_turn(i)
                for s in range(4):
                    project(q + 1, s, hThi, hTlo, 2, f_half, None if first else (gu_done, 2 * i - 1))
                    if with_mod and s == 2:
                        reduce(GT_F - 1 + i, 0)
                    if tail and s == 0:
                        spread(diag3, 0, 4, 4)
                    if tail and s == 2:
                        pe.wait_ge(grow_done, 6)
                        spread(diag3, 1, 4, 4)

            f1(0, True, False, False)
            with pe.Fori(1, 5) as i:
                f1(i, False, True, False)
            with pe.Fori(5, FB - 1) as i:
                f1(i, False, False, False)
            f1(FB - 1, False, False, True)
            gu_turn(FB)

            def f2(i, first, end):
                def hidden_ready(s):
                    pe.wait_ge(gk_hi, 4 * i + s + 1)
                    pe.wait_ge(gk_lo, 4 * i + s + 1)
                    split_ready(G_F2 // 4 + i, s)

                def part(s, b):
                    tok = slice(b * P, (b + 1) * P)
                    for n in range(NB):
                        if first and s == 0 and b == 0 and n == 0:
                            pe.wait_ge(silu_done, 2 * FB)
                        if first and s == 0 and b == 0 and n == 2:
                            pe.wait_ge(gu_done, 2 * FB)
                        if first and s == 0 and b == 1 and n == 0:
                            pe.wait_ge(grow_done, 8)
                        if first and s == 0 and b == 1 and n == 2:
                            pe.wait_ge(guT_done, 2 * FB)
                        last = three(ps[:, 4 * b + n], hThi[:, s, tok], hTlo[:, s, tok], s, n,
                                     first and s == 0, end and s == 3)
                        if end and s == 3:
                            last.then_inc(y2_bank, 1)
                    return last

                for s in range(4):
                    hidden_ready(s)
                    for b in range(HB):
                        last = part(s, b)
                    if not (end and s == 3):
                        last.then_inc(pe_done, 1)

            f2(0, True, False)
            with pe.Fori(1, FT // 4 - 1) as i:
                f2(i, False, False)
            f2(FT // 4 - 1, False, True)


SETUP_ANGLES = 17
ATT_LO = (3, 1, 1, 1)
POOL_ADDS = (3, 2)
F_MOD = [(0, 1), (2,), (3,), (4, 5), (6,), (7,), (), ()]
H2_STEPS = [(0, 0), (0, 1), (1, 0), (1, 1), (0, 2), (1, 2), (0, 3), (1, 3)]
H2_BANKS = [4, 5, 6, 7, 2, 3, 4, 5]


def kernel(**inputs):
    import numpy as np
    import concourse.bacc as bacc
    from concourse import mybir as mb
    from concourse.bass_utils import run_bass_kernel_spmd as run

    def cols(a):
        return np.ascontiguousarray(a.reshape(-1, P).T)

    x = np.ascontiguousarray(inputs["x"])[0]
    gains = np.stack([cols(inputs["norm_g"][0, n]) for n in range(4)], axis=1)
    power = np.arange(0, HD, 2, dtype=np.float32) / np.float32(HD)
    invf = (np.float32(1.0) / np.power(np.float32(10000.0), power)).astype(np.float32)
    sinks = np.asarray(inputs["swa_sinks"])[0].reshape(4, 2, 2, 2).transpose(0, 1, 3, 2)
    sinks = np.repeat(sinks[:, :, None], HB, axis=2).reshape(1, 2 * QH)
    arrays = {
        "x": x,
        "cT": cols(inputs["c"][0]),
        "pos": np.ascontiguousarray(np.asarray(inputs["positions"])[0].reshape(HB, P).T),
        "invf": np.ascontiguousarray(np.broadcast_to(invf, (P, HALF))),
        "mod_w": np.ascontiguousarray(inputs["mod_w"][0]),
        "modbT": cols(inputs["mod_b"][0]),
        "gT": np.ascontiguousarray(gains),
        "w_qkv": np.ascontiguousarray(inputs["swa_w_qkv"][0]),
        "w_o": np.ascontiguousarray(inputs["swa_w_o"][0]),
        "sinks": np.ascontiguousarray(np.broadcast_to(sinks, (P, 2 * QH))),
        "w_in": np.ascontiguousarray(inputs["ffn_w_in"][0]),
        "w_out": np.ascontiguousarray(inputs["ffn_w_out"][0]),
    }
    nc = bacc.Bacc("TRN2", target_bir_lowering=False, num_devices=1)
    feed, args = {}, []
    for name, a in arrays.items():
        feed[f"in_{name}"] = a
        args.append(nc.dram_tensor(f"in_{name}", a.shape, mb.dt.from_np(a.dtype), kind="ExternalInput").ap())
    args.append(nc.dram_tensor("out_0", (T, D), mb.dt.float32, kind="ExternalOutput").ap())
    build(nc, *args)
    r = run(nc, [feed], core_ids=[0])
    return r.results[0]["out_0"].reshape(1, T, D)
```
